# Optimizing a Trainium2 kernel written in Bass

```python
import jax, jax.numpy as jnp
from jax import lax
import numpy as np

D_MODEL = 1024
BATCH = 1
SEQ = 1024
DEPTH = 2

CHUNK = 64
HEAD_DIM = 64
N_MIXERS = 2
SWA_Q_HEADS = 16
SWA_KV_HEADS = 4
SWA_WINDOW = 128
SWA_WIN_CHUNKS = SWA_WINDOW // CHUNK
FOX_HEADS = 16
FOX_QBLOCK = 128
D_FF = -(-8 * D_MODEL // (3 * 256)) * 256
ROPE_THETA = 10000.0
RMS_EPS = 1e-6
NEG_INF = -1e30
N_A_LAYERS = (DEPTH + 1) // 2
N_B_LAYERS = DEPTH // 2

kernel_name = "hybrid_swa_sink_fox_trunk"

def _rmsnorm(x, g):
    xf = x.astype(jnp.float32)
    y = xf * lax.rsqrt(jnp.mean(xf * xf, axis=-1, keepdims=True) + RMS_EPS)
    return (y * g.astype(jnp.float32)).astype(x.dtype)

def _rope_tables(seq_len):
    half = HEAD_DIM // 2
    inv_freq = ROPE_THETA ** (-jnp.arange(half, dtype=jnp.float32) / half)
    ang = jnp.arange(seq_len, dtype=jnp.float32)[:, None] * inv_freq[None, :]
    return jnp.cos(ang), jnp.sin(ang)

def _rope(t, cos, sin):
    half = HEAD_DIM // 2
    tf = t.astype(jnp.float32)
    t1, t2 = tf[..., :half], tf[..., half:]
    c = cos[None, :, None, :]
    s = sin[None, :, None, :]
    return jnp.concatenate([t1 * c - t2 * s, t2 * c + t1 * s], axis=-1).astype(t.dtype)

def _chunk_band(t, n_back):
    pad = ((0, 0),) * (t.ndim - 2)
    parts = []
    for p in range(n_back, 0, -1):
        parts.append(jnp.pad(t, ((0, 0), (p, 0)) + pad)[:, :-p])
    parts.append(t)
    return jnp.concatenate(parts, axis=2)

def _swa_sink_mixer(h, w_in, sinks, w_out, cos, sin):
    B, S, _ = h.shape
    nc = S // CHUNK
    G = SWA_Q_HEADS // SWA_KV_HEADS
    n_back = SWA_WIN_CHUNKS - 1
    qkv = h @ w_in
    q, k, v = jnp.split(qkv, [SWA_Q_HEADS * HEAD_DIM, (SWA_Q_HEADS + SWA_KV_HEADS) * HEAD_DIM], axis=-1)
    q = _rope(q.reshape(B, S, SWA_Q_HEADS, HEAD_DIM), cos, sin)
    k = _rope(k.reshape(B, S, SWA_KV_HEADS, HEAD_DIM), cos, sin)
    v = v.reshape(B, S, SWA_KV_HEADS, HEAD_DIM)
    q = q.reshape(B, nc, CHUNK, SWA_KV_HEADS, G, HEAD_DIM)
    kb = _chunk_band(k.reshape(B, nc, CHUNK, SWA_KV_HEADS, HEAD_DIM), n_back)
    vb = _chunk_band(v.reshape(B, nc, CHUNK, SWA_KV_HEADS, HEAD_DIM), n_back)
    logits = jnp.einsum('bcqhgd,bckhd->bchgqk', q, kb,
                        preferred_element_type=jnp.float32) * (HEAD_DIM ** -0.5)
    back = n_back - jnp.arange(SWA_WIN_CHUNKS * CHUNK) // CHUNK
    valid = jnp.arange(nc)[:, None] >= back[None, :]
    logits = jnp.where(valid[None, :, None, None, None, :], logits, NEG_INF)
    sink = jnp.broadcast_to(sinks.astype(jnp.float32).reshape(1, 1, SWA_KV_HEADS, G, 1, 1),
                            logits.shape[:-1] + (1,))
    probs = jax.nn.softmax(jnp.concatenate([logits, sink], axis=-1), axis=-1)[..., :-1]
    o = jnp.einsum('bchgqk,bckhd->bcqhgd', probs.astype(vb.dtype), vb)
    return o.reshape(B, S, SWA_Q_HEADS * HEAD_DIM) @ w_out

def _fox_mixer(h, w_in, f_bias, w_out):
    B, S, _ = h.shape
    HD = FOX_HEADS * HEAD_DIM
    nq = S // FOX_QBLOCK
    proj = h @ w_in
    q, k, v, f_logit = jnp.split(proj, [HD, 2 * HD, 3 * HD], axis=-1)
    q = q.reshape(B, S, FOX_HEADS, HEAD_DIM)
    k = k.reshape(B, S, FOX_HEADS, HEAD_DIM)
    v = v.reshape(B, S, FOX_HEADS, HEAD_DIM)
    log_f = jax.nn.log_sigmoid(f_logit.astype(jnp.float32) + f_bias.astype(jnp.float32))
    cum = jnp.cumsum(log_f, axis=1)
    cum_k = cum.transpose(0, 2, 1)
    q_blocks = q.reshape(B, nq, FOX_QBLOCK, FOX_HEADS, HEAD_DIM).transpose(1, 0, 2, 3, 4)
    c_blocks = cum.reshape(B, nq, FOX_QBLOCK, FOX_HEADS).transpose(1, 0, 3, 2)
    k_pos = jnp.arange(S)
    scale = HEAD_DIM ** -0.5

    def block(args):
        qb, cb, i = args
        s = jnp.einsum('bqhd,bkhd->bhqk', qb, k, preferred_element_type=jnp.float32) * scale
        s = s + cb[..., None] - cum_k[:, :, None, :]
        q_pos = i * FOX_QBLOCK + jnp.arange(FOX_QBLOCK)
        s = jnp.where((k_pos[None, :] <= q_pos[:, None])[None, None], s, NEG_INF)
        p = jax.nn.softmax(s, axis=-1)
        return jnp.einsum('bhqk,bkhd->bqhd', p.astype(v.dtype), v)

    o = lax.map(block, (q_blocks, c_blocks, jnp.arange(nq)))
    o = o.transpose(1, 0, 2, 3, 4).reshape(B, S, HD)
    return o @ w_out

def _swiglu(h, w_gate_up, w_down):
    gu = h @ w_gate_up
    g, u = jnp.split(gu, 2, axis=-1)
    return (jax.nn.silu(g) * u) @ w_down

def setup_inputs(seed: int = 0) -> dict:
    key = jax.random.key(seed)
    ks = jax.random.split(key, 16)
    f32 = jnp.float32
    D = D_MODEL
    swa_in_w = (SWA_Q_HEADS + 2 * SWA_KV_HEADS) * HEAD_DIM
    fox_in_w = 3 * FOX_HEADS * HEAD_DIM + FOX_HEADS
    x = jax.random.normal(ks[0], (BATCH, SEQ, D), f32)
    norm_mix = 1.0 + 0.05 * jax.random.normal(ks[1], (DEPTH, D), f32)
    norm_ffn = 1.0 + 0.05 * jax.random.normal(ks[2], (DEPTH, D), f32)
    swa_w_in = jax.random.normal(ks[3], (N_A_LAYERS, D, swa_in_w), f32) * D ** -0.5
    swa_sinks = jax.random.normal(ks[4], (N_A_LAYERS, SWA_Q_HEADS), f32)
    swa_w_out = jax.random.normal(ks[5], (N_A_LAYERS, SWA_Q_HEADS * HEAD_DIM, D), f32) * (SWA_Q_HEADS * HEAD_DIM) ** -0.5
    fox_w_in = jax.random.normal(ks[6], (N_B_LAYERS, D, fox_in_w), f32) * D ** -0.5
    fox_f_bias = (jnp.linspace(1.0, 6.0, FOX_HEADS, dtype=f32)[None, :]
                  + 0.1 * jax.random.normal(ks[7], (N_B_LAYERS, FOX_HEADS), f32))
    fox_w_out = jax.random.normal(ks[8], (N_B_LAYERS, FOX_HEADS * HEAD_DIM, D), f32) * (FOX_HEADS * HEAD_DIM) ** -0.5
    ffn_w_gate_up = jax.random.normal(ks[9], (DEPTH, D, 2 * D_FF), f32) * D ** -0.5
    ffn_w_down = jax.random.normal(ks[10], (DEPTH, D_FF, D), f32) * D_FF ** -0.5
    norm_final = 1.0 + 0.05 * jax.random.normal(ks[11], (D,), f32)
    return {"x": x, "norm_mix": norm_mix, "norm_ffn": norm_ffn,
            "swa_w_in": swa_w_in, "swa_sinks": swa_sinks, "swa_w_out": swa_w_out,
            "fox_w_in": fox_w_in, "fox_f_bias": fox_f_bias, "fox_w_out": fox_w_out,
            "ffn_w_gate_up": ffn_w_gate_up, "ffn_w_down": ffn_w_down,
            "norm_final": norm_final}

def reference(x, norm_mix, norm_ffn, swa_w_in, swa_sinks, swa_w_out,
              fox_w_in, fox_f_bias, fox_w_out, ffn_w_gate_up, ffn_w_down, norm_final):
    cos, sin = _rope_tables(x.shape[1])
    for i in range(DEPTH):
        h = _rmsnorm(x, norm_mix[i])
        j = i // N_MIXERS
        if i % N_MIXERS == 0:
            mix = _swa_sink_mixer(h, swa_w_in[j], swa_sinks[j], swa_w_out[j], cos, sin)
        else:
            mix = _fox_mixer(h, fox_w_in[j], fox_f_bias[j], fox_w_out[j])
        x = x + mix.astype(x.dtype)
        h = _rmsnorm(x, norm_ffn[i])
        x = x + _swiglu(h, ffn_w_gate_up[i], ffn_w_down[i]).astype(x.dtype)
    return _rmsnorm(x, norm_final)


_drawn_inputs = setup_inputs


def setup_inputs(seed=0):
    import zlib

    import numpy as np

    out = dict(_drawn_inputs(seed))
    spreads = {}
    factors = {'swa_sinks': 8.0}
    for name, (base, spread) in spreads.items():
        noise = np.random.default_rng([zlib.crc32(name.encode()), seed]).standard_normal(out[name].shape)
        drawn = base * np.exp(spread * noise) if base else spread * noise
        out[name] = __import__('jax').numpy.asarray(drawn.astype(out[name].dtype))
    for name, factor in factors.items():
        out[name] = (out[name] * factor).astype(out[name].dtype)
    return out
```

```python
import numpy as np
from contextlib import ExitStack

import concourse.bass as bass
from concourse import mybir

FP32 = mybir.dt.float32
F32R = mybir.dt.float32r
BF16 = mybir.dt.bfloat16
ALU = mybir.AluOpType
ACT = mybir.ActivationFunctionType
AX = mybir.AxisListType

P = 128
SEQ = 1024
D = 1024
KD = D // P
TT = SEQ // P
HALF = SEQ // 2
HD = 64
CHUNK = 64
SWA_Q, SWA_KV = 16, 4
GQ = SWA_Q // SWA_KV
FOX_H = 16
D_FF = 2816
FT = D_FF // P
FF_GROUPS = (8, 7, 7)
SWA_IN = (SWA_Q + 2 * SWA_KV) * HD // P
FOX_IN = 3 * FOX_H * HD // P
EPS = 1e-6
SCALE = HD ** -0.5
BIG = 1e30


def trunk(nc, x, norm_mix, norm_ffn, swa_w_in, swa_sinks, swa_w_out, fox_w_in, fox_f_bias, fox_w_out,
          w_gate_up, w_down, norm_final, rope, masks, out):
    ctx = ExitStack()
    with ctx:
        base = (nc.sbuf_base + 63) // 64 * 64

        def at(name, kib, shape, dt=FP32):
            return nc.alloc_sbuf_tensor_at(name, shape, dt, offset=base + int(kib * 1024))

        x_t = at("x_t", 0, [P, KD, SEQ])
        fox_p_hi = [at(f"fox_p_hi{i}", 16 * i, [P, TT, 2 * P], F32R) for i in range(2)]
        fox_p_lo = [at(f"fox_p_lo{i}", 16 * i + 8, [P, TT, 2 * P], F32R) for i in range(2)]
        swa_p_hi = [at(f"swa_p_hi{i}", 8 * i, [P, 2, GQ * P], F32R) for i in range(2)]
        swa_p_lo = [at(f"swa_p_lo{i}", 8 * i + 4, [P, 2, GQ * P], F32R) for i in range(2)]
        h_hi = at("h_hi", 32, [P, KD, SEQ], F32R)
        h_lo = at("h_lo", 64, [P, KD, SEQ], F32R)
        x_fin = at("x_fin", 32, [P, KD, SEQ])
        score = [at(f"score{i}", 32 + 4 * i, [P, SEQ]) for i in range(4)]
        v_hi = [at(f"v_hi{i}", 48 + 8 * i, [P, TT, P], F32R) for i in range(2)]
        v_lo = [at(f"v_lo{i}", 52 + 8 * i, [P, TT, P], F32R) for i in range(2)]
        fox_q_hi = [at(f"fox_q_hi{i}", 64 + 12 * i, [P, SEQ], F32R) for i in range(2)]
        fox_q_lo = [at(f"fox_q_lo{i}", 68 + 12 * i, [P, SEQ], F32R) for i in range(2)]
        fox_k = [at(f"fox_k{i}", 72 + 12 * i, [P, SEQ], F32R) for i in range(2)]
        fox_first = [at("fox_first_q_hi", 112, [P, SEQ], F32R), at("fox_first_q_lo", 116, [P, SEQ], F32R),
                     at("fox_first_k", 120, [P, SEQ], F32R), at("fox_first_v_hi", 124, [P, TT, P], F32R),
                     at("fox_first_v_lo", 156, [P, TT, P], F32R)]
        swa_q_hi = [at("swa_q_hi0", 16, [P, 2, SEQ], F32R), at("swa_q_hi1", 64, [P, 2, SEQ], F32R)]
        swa_q_lo = [at("swa_q_lo0", 24, [P, 2, SEQ], F32R), at("swa_q_lo1", 72, [P, 2, SEQ], F32R)]
        swa_k_hi = [at("swa_k_hi0", 192, [P, SEQ], F32R), at("swa_k_hi1", 80, [P, SEQ], F32R)]
        swa_k_lo = [at("swa_k_lo0", 196, [P, SEQ], F32R), at("swa_k_lo1", 84, [P, SEQ], F32R)]
        o_hi = at("o_hi", 96, [P, KD, SEQ], F32R)
        o_lo = at("o_lo", 128, [P, KD, SEQ], F32R)
        hid_hi = at("hid_hi", 96, [P, 8, SEQ], F32R)
        hid_lo = at("hid_lo", 128, [P, 8, SEQ], F32R)
        rope_cos = at("rope_cos", 96, [P, SEQ])
        rope_sin = at("rope_sin", 100, [P, SEQ])
        rope_part = at("rope_part", 116, [P, SEQ])
        start_sq = at("start_sq", 104, [P, KD, P])
        start_x = [at(f"start_x{i}", 108 + 4 * i, [P, D]) for i in range(2)]
        gate = [at(f"gate{i}", 96 + 4 * i, [FOX_H, SEQ]) for i in range(8)]
        out_tile = [at(f"out_tile{i}", 96 + 4 * i, [P, D]) for i in range(2)]
        w_raw = [at(f"w_raw{i}", 160 + 4 * i, [P, KD, P]) for i in range(2)]
        w_hi = [at(f"w_hi{i}", 168 + 4 * i, [P, KD, P], F32R) for i in range(2)]
        w_lo = [at(f"w_lo{i}", 176 + 4 * i, [P, KD, P], F32R) for i in range(2)]
        rstd = at("rstd", 184, [P, SEQ])
        ssq = at("ssq", 188, [P, SEQ])
        work_a = at("work_a", 192, [P, SEQ])
        work_b = at("work_b", 196, [P, SEQ])
        work_c = at("work_c", 200, [P, SEQ])
        diag = at("diag", 196, [P, TT, P])
        sq = [at(f"sq{i}", 192 + 2 * i, [P, HALF]) for i in range(2)]
        cum_all = [at(f"cum_all{i}", 192 + 4 * i, [P, SEQ]) for i in range(2)]
        small_at = [204 * 1024]

        def small(name, shape, dt=FP32):
            size = int(np.prod(shape[1:])) * (2 if dt == BF16 else 4)
            t = nc.alloc_sbuf_tensor_at(name, shape, dt, offset=base + small_at[0], align_bytes=8)
            small_at[0] += (size + 7) // 8 * 8
            assert base + small_at[0] <= nc.sbuf_usable_end
            return t

        ident = small("ident", [P, P])
        ident_bf = small("ident_bf", [P, P], BF16)
        causal_bf = small("causal_bf", [P, P], BF16)
        band = small("band", [P, 2, P])
        ones = small("ones", [P, P])
        gains = small("gains", [P, 5, KD])
        sinks = small("sinks", [P, SWA_Q])
        f_bias = small("f_bias", [FOX_H, 1])
        nat_v = small("nat_v", [P, TT])
        nat_y = small("nat_y", [P, TT])
        nat_t = small("nat_t", [P, TT])
        neg_max = [small(f"neg_max{i}", [P, GQ]) for i in range(4)]
        psum_l = [small(f"psum_l{i}", [P, GQ]) for i in range(4)]
        sink_e = [small(f"sink_e{i}", [P, GQ]) for i in range(4)]
        inv_l = [small(f"inv_l{i}", [P, GQ]) for i in range(4)]
        eps_c = small("eps_c", [P, 1])
        part_hi = [at(f"part_hi{i}", 136 + 4 * i, [P, SEQ], F32R) for i in range(2)]
        part_lo = [at(f"part_lo{i}", 144 + 4 * i, [P, SEQ], F32R) for i in range(2)]
        wf_lo = at("wf_lo", 128, [P, KD, FOX_H], F32R)
        wf_raw = at("wf_raw", 129, [P, KD, FOX_H])
        wf_hi = at("wf_hi", 130, [P, KD, FOX_H], F32R)
        causal = at("causal", 131, [P, P])

        psum = nc.alloc_psum_tensor("psum", [P, 8 * HALF], FP32)
        bank = [psum[:, i * HALF:(i + 1) * HALF] for i in range(8)]

        x_scr = nc.dram_tensor("x_scr", [P, KD, SEQ], FP32).ap()
        swa_qk = [nc.dram_tensor(f"swa_qk_{w}", [(SWA_Q + SWA_KV) * HD, SEQ], FP32).ap() for w in ("hi", "lo")]
        swa_v = [nc.dram_tensor(f"swa_v_{w}", [SWA_KV // 2, P, TT, P], FP32).ap() for w in ("hi", "lo")]
        fox_qk = [nc.dram_tensor(f"fox_qk_{w}", [2 * FOX_H * HD, SEQ], FP32).ap() for w in ("hi", "lo")]
        fox_v = [nc.dram_tensor(f"fox_v_{w}", [FOX_H // 2, P, TT, P], FP32).ap() for w in ("hi", "lo")]
        cum_scr = nc.dram_tensor("cum_scr", [FOX_H, SEQ], FP32).ap()

        def sem(name):
            return ctx.enter_context(nc.semaphore(name))

        w_loaded = [sem(f"w_loaded{i}") for i in range(2)]
        w_high = sem("w_high")
        w_split = sem("w_split")
        mm_done = sem("mm_done")
        evac_done = sem("evac_done")
        const_in = sem("const_in")
        rope_in = sem("rope_in")
        const_ready = sem("const_ready")
        xin_loaded = [sem(f"xin_loaded{i}") for i in range(2)]
        xin_t = sem("xin_t")
        start_copy = sem("start_copy")
        start_gain = sem("start_gain")
        start_hi = sem("start_hi")
        start_sum = sem("start_sum")
        h_ready = sem("h_ready")
        hi_done = sem("hi_done")
        sq_done = sem("sq_done")
        sq_used = sem("sq_used")
        nat_done = sem("nat_done")
        sd_done = sem("sd_done")
        newton = sem("newton")
        diag_done = sem("diag_done")
        bc_done = sem("bc_done")
        rstd_ready = sem("rstd_ready")
        swapped = sem("swapped")
        cos_done = sem("cos_done")
        sin_done = sem("sin_done")
        c_ready = sem("c_ready")
        part_high = sem("part_high")
        part_low = sem("part_low")
        value_high = sem("value_high")
        part_t = sem("part_t")
        stored = [sem(f"stored{i}") for i in range(2)]
        gate_in = sem("gate_in")
        gate_w = sem("gate_w")
        gate_mm = sem("gate_mm")
        gate_v = sem("gate_v")
        gate_a = sem("gate_a")
        gate_stored = sem("gate_stored")
        silu_done = sem("silu_done")
        prod_done = sem("prod_done")
        hid_hi_done = sem("hid_hi_done")
        hid_ready = sem("hid_ready")
        x_stored = sem("x_stored")
        x_back = [sem(f"x_back{i}") for i in range(4)]
        out_ready = sem("out_ready")
        out_t = sem("out_t")
        out_stored = [sem(f"out_stored{i}") for i in range(2)]

        C_A0 = 0
        C_O0 = C_A0 + SWA_IN
        C_F0 = C_O0 + KD
        C_A1 = C_F0 + 2 * FT + KD * len(FF_GROUPS)
        C_O1 = C_A1 + FOX_IN
        C_F1 = C_O1 + KD
        C_END = C_F1 + 2 * FT + KD * len(FF_GROUPS)

        def wait(eng, s, value):
            if not (isinstance(value, int) and value <= 0):
                eng.wait_ge(s, value)

        def ff_phases(c0):
            c, t, found = c0, 0, []
            for n in FF_GROUPS:
                found.append((c, c + 2 * n, t, n))
                c, t = c + 2 * n + KD, t + n
            return found

        def half(h):
            return slice(h * HALF, (h + 1) * HALF)

        def apart(eng):
            eng.nop(nofuse=True)

        block = ctx.enter_context(nc.Block())

        class Attention:
            def __init__(self, name):
                self.fox = name == "fox"
                self.units = FOX_H if self.fox else SWA_KV
                self.qk, self.v = (fox_qk, fox_v) if self.fox else (swa_qk, swa_v)
                self.qk_dmas, self.v_dmas = (5, 2) if self.fox else (6, 4)
                self.qk_in = [sem(f"{name}_qk_in{e}") for e in range(2)]
                self.v_in = [sem(f"{name}_v_in{e}") for e in range(2)]
                self.qk_done = sem(f"{name}_qk_done")
                self.max_done = sem(f"{name}_max_done")
                self.exp_done = sem(f"{name}_exp_done")
                self.sum_done = sem(f"{name}_sum_done")
                self.inv_done = sem(f"{name}_inv_done")
                self.norm_done = sem(f"{name}_norm_done")
                self.t_done = sem(f"{name}_t_done")
                self.ph_done = sem(f"{name}_ph_done")
                self.t_free = sem(f"{name}_t_free")
                self.pv_done = sem(f"{name}_pv_done")
                self.oh_done = sem(f"{name}_oh_done")
                self.o_free = sem(f"{name}_o_free")
                self.tiles = [(0, 1), (2, 3), (4,), (5,), (6,), (7,)] if self.fox else [(t,) for t in range(TT)]
                self.steps = len(self.tiles)
                self.blocks = [[[(0, 0, 1), (1, 0, 2)]], [[(2, 0, 3)], [(3, 0, 4)]]] + \
                    [[[(t, 0, 4)], [(t, 4, t - 3)]] for t in range(4, TT)] if self.fox else [[0, 1]] * TT
                self.fills = [len(b) for b in self.blocks]
                self.unit_fills = sum(self.fills)
                self.groups = TT // 2 if self.fox else TT
                n = 2 * self.unit_fills
                self.turns = [T_BANKS[i % 3] for i in range(n)]
                if n % 3 == 1:
                    self.turns[-1] = T_BANKS[1]

            def count(self, u, s):
                return self.steps * u + s

            def ring(self, e, s):
                return (self.steps * e + s) % 4

            def fill(self, u, s):
                return self.unit_fills * u + sum(self.fills[:s])

            def bank_of(self, u, e, s, j):
                f = self.fill(u if isinstance(u, int) else e, s) + j
                n = len(self.turns)
                ago = next(d for d in range(1, n) if self.turns[(f - d) % n] == self.turns[f % n])
                return bank[self.turns[f % n]], ago

            def group(self, s):
                return self.tiles[s][-1] // 2 if self.fox else s

            def completes(self, s):
                return not self.fox or self.tiles[s][-1] % 2 == 1

        T_BANKS = (4, 5, 7)
        O_BANK = 6
        swa, fox = Attention("swa"), Attention("fox")
        cum_in = [sem(f"fox_cum_in{e}") for e in range(2)]
        swa_row = sem("swa_row")
        N_CONST = 9
        GATE_STEPS = 14

        def a_step(a, pi, i, last):
            if i < 2 * a.steps:
                return 2 * pi + i // a.steps, i // a.steps, i % a.steps
            return None if last else (2 * pi + 2, 0, i - 2 * a.steps)

        def a_done(a, pi, i, first):
            if i == 0:
                return None if first else (2 * pi - 1, 1, a.steps - 1, pi - 1)
            e, s = (i - 1) // a.steps, (i - 1) % a.steps
            return (2 * pi + e, e, s, pi) if a.completes(s) else None

        def cols(t, a, n=P):
            return t[:, a:a + n]

        def rows(e):
            return slice(e * HD, (e + 1) * HD)

        def fox_w(t):
            return (t + 1) * P

        def fox_at(t):
            return {1: P, 3: HALF}.get(t, 0)

        def fox_pieces(blocks, tb, p):
            at0, found = 0, []
            for t, k, n in blocks:
                found.append((p[:, k:k + n, t % 2 * P:t % 2 * P + P],
                              tb[:, at0:at0 + n * P].rearrange("p (b q) -> p b q", q=P)))
                at0 += n * P
            return found

        def fox_operands(u, e):
            if isinstance(u, int) and u == 0:
                return fox_first
            return [b[e] for b in (fox_q_hi, fox_q_lo, fox_k, v_hi, v_lo)]

        w_in_view = {"swa": swa_w_in[0].rearrange("(k p) n -> p k n", p=P),
                     "fox": fox_w_in[0].rearrange("(k p) n -> p k n", p=P)}
        w_out_view = {"swa": swa_w_out[0].rearrange("(k p) n -> p k n", p=P),
                      "fox": fox_w_out[0].rearrange("(k p) n -> p k n", p=P)}
        gu_view = [w_gate_up[i].rearrange("(k p) n -> p k n", p=P) for i in range(2)]
        dn_view = [w_down[i].rearrange("(k p) n -> p k n", p=P) for i in range(2)]
        x_view = x[0].rearrange("(t p) d -> t p d", p=P)
        out_view = out[0].rearrange("(t p) d -> t p d", p=P)

        @block.sync
        def _(sp):
            def load_w(c, p, src, n=KD):
                wait(sp, w_split, c - 1)
                sp.dma_start(w_raw[p][:, 0:n, :], src).then_inc(w_loaded[p], 16)

            def strip(view, m):
                return view[:, :, bass.ds(m * P, P)]

            def load_out_w(c0, view, i):
                for p in range(2):
                    load_w(c0 + 2 * i + p, p, strip(view, 2 * i + p))

            def load_qk(a, u, e):
                hi, lo = a.qk
                wait(sp, a.qk_done, a.steps * (u - 1))
                if a.fox:
                    q_hi, q_lo, k = fox_operands(u, e)[:3]
                    for r in range(2):
                        sp.dma_start(q_hi[rows(r), :].bitcast(FP32), hi[bass.ds(u * HD, HD), :]).then_inc(a.qk_in[e], 16)
                        sp.dma_start(k[rows(r), :].bitcast(FP32), a.qk[r][bass.ds((FOX_H + u) * HD, HD), :])\
                            .then_inc(a.qk_in[e], 16)
                    sp.dma_start(q_lo[rows(0), :].bitcast(FP32), lo[bass.ds(u * HD, HD), :]).then_inc(a.qk_in[e], 16)
                    wait(sp, a.max_done, a.steps * (u - 1))
                    sp.dma_start(cum_all[e][:, :], cum_scr[bass.ds(u, 1), :].to_broadcast([P, SEQ])).then_inc(cum_in[e], 16)
                    return
                for src, q_dst, k_dst in ((hi, swa_q_hi, swa_k_hi), (lo, swa_q_lo, swa_k_lo)):
                    sp.dma_start(q_dst[e][:, :, :].bitcast(FP32),
                                 src[2 * u * P:(2 * u + 2) * P, :].rearrange("(a p) n -> p a n", p=P))\
                        .then_inc(a.qk_in[e], 16)
                    for r in range(2):
                        sp.dma_start(k_dst[e][rows(r), :].bitcast(FP32),
                                     src[(SWA_Q + u) * HD:(SWA_Q + u + 1) * HD, :]).then_inc(a.qk_in[e], 16)

            def load_v(a, u, e, pi):
                wait(sp, a.pv_done, a.groups * (u - 1))
                if a.fox:
                    for src, dst in zip(a.v, fox_operands(u, e)[3:]):
                        sp.dma_start(dst[:, :, :].bitcast(FP32),
                                     src[bass.ds(pi, 1)].rearrange("a p t d -> (a p) t d"))\
                            .then_inc(a.v_in[e], 16)
                    return
                for src, dst in zip(a.v, (v_hi, v_lo)):
                    for r in range(2):
                        sp.dma_start(dst[e][:, :, rows(r)].bitcast(FP32), src[u // 2, :, :, rows(u % 2)])\
                            .then_inc(a.v_in[e], 16)

            def load_unit(a, u, e, pi):
                load_qk(a, u, e)
                load_v(a, u, e, pi)

            def load_ffn(layer, c0):
                for cg, cd, t0, n in ff_phases(c0):
                    with sp.Fori(0, n) as j:
                        load_w(cg + 2 * j, 0, strip(gu_view[layer], t0 + j))
                        load_w(cg + 2 * j + 1, 1, strip(gu_view[layer], FT + t0 + j))
                    with sp.Fori(0, KD // 2) as i:
                        for p in range(2):
                            load_w(cd + 2 * i + p, p,
                                   dn_view[layer][:, t0:t0 + n, bass.ds((2 * i + p) * P, P)], n)

            def attention_loads(a):
                if a.fox:
                    sp.wait_ge(gate_stored, 16)
                    sp.wait_ge(stored[0], 16 * SWA_IN + 32 * (FOX_H + 2) // 2)
                    load_unit(a, 0, 0, 0)
                else:
                    for p in range(2):
                        sp.wait_ge(stored[p], 16 * (SWA_IN - 2))
                    sp.wait_ge(x_stored, 16)
                    load_qk(a, 0, 0)
                sp.wait_ge(mm_done, 2 * (C_O1 if a.fox else C_O0))
                for p in range(2):
                    sp.wait_ge(stored[p], 16 * (SWA_IN + (FOX_IN if a.fox else 0)))
                if not a.fox:
                    load_v(a, 0, 0, 0)
                load_unit(a, 1, 1, 0)
                if a.fox:
                    with sp.Fori(1, a.units // 2) as pi:
                        for e in range(2):
                            load_unit(a, 2 * pi + e, e, pi)
                else:
                    for u in range(2, a.units):
                        load_unit(a, u, u % 2, u // 2)
                sp.wait_ge(a.pv_done, a.groups * a.units)
                k = 2 if a.fox else 0
                sp.dma_start(x_t[:, 0:2, :], x_scr[:, 0:2, :]).then_inc(x_back[k], 16)
                sp.dma_start(x_t[:, 2:KD, :], x_scr[:, 2:KD, :]).then_inc(x_back[k + 1], 16)

            sp.dma_start(ident[:, :], masks[:, 0:P]).then_inc(const_in, 16)
            sp.dma_start(start_x[0][:, :], x_view[0]).then_inc(xin_loaded[0], 16)
            sp.dma_start(gains[:, 0:1, :], norm_mix[0:1].rearrange("a (k p) -> p a k", p=P), allow_slow_non_contiguous=True).then_inc(const_in, 16)
            sp.dma_start(start_x[1][:, :], x_view[1]).then_inc(xin_loaded[1], 16)
            load_w(0, 0, strip(w_in_view["swa"], 0))
            load_w(1, 1, strip(w_in_view["swa"], 1))
            for t in range(2, TT):
                sp.wait_ge(xin_t, t - 1)
                sp.dma_start(start_x[t % 2][:, :], x_view[t]).then_inc(xin_loaded[t % 2], 16)
            sp.dma_start(rope_cos[:, :], rope[0]).then_inc(rope_in, 16)
            sp.dma_start(rope_sin[:, :], rope[1]).then_inc(rope_in, 16)

            with sp.Fori(1, SWA_IN // 2) as i:
                for p in range(2):
                    load_w(2 * i + p, p, strip(w_in_view["swa"], 2 * i + p))
            load_out_w(C_O0, w_out_view["swa"], 0)
            attention_loads(swa)
            with sp.Fori(1, KD // 2) as i:
                load_out_w(C_O0, w_out_view["swa"], i)
            load_ffn(0, C_F0)

            load_w(C_A1, 0, strip(w_in_view["fox"], 0))
            load_w(C_A1 + 1, 1, strip(w_in_view["fox"], 1))
            sp.wait_ge(mm_done, 2 * C_A1)
            f0 = 3 * FOX_H * HD
            sp.dma_start(wf_raw[:, :, :], w_in_view["fox"][:, :, f0:f0 + FOX_H]).then_inc(gate_in, 16)
            sp.dma_start(f_bias[:, :], fox_f_bias.rearrange("a h -> h a"), allow_slow_non_contiguous=True).then_inc(gate_in, 16)
            with sp.Fori(1, FOX_IN // 2) as i:
                for p in range(2):
                    load_w(C_A1 + 2 * i + p, p, strip(w_in_view["fox"], 2 * i + p))
            load_out_w(C_O1, w_out_view["fox"], 0)
            attention_loads(fox)
            with sp.Fori(1, KD // 2) as i:
                load_out_w(C_O1, w_out_view["fox"], i)
            load_ffn(1, C_F1)
            for p in range(2):
                sp.wait_ge(out_stored[p], 16 * TT // 2)

        @block.gpsimd
        def _(pool):
            nc.gpsimd.memset(ones[:, :], 1.0).then_inc(const_ready, 1)

            def norm_probs(a, u, e, s):
                n = a.count(u, s)
                sl = a.ring(e, s)
                pool.wait_ge(a.inv_done, n + 1)
                if a.fox:
                    for i, t in enumerate(a.tiles[s]):
                        sc = score[sl][:, fox_at(t):fox_at(t) + fox_w(t)]
                        last = nc.gpsimd.tensor_tensor(sc, sc, inv_l[sl][:, i:i + 1].to_broadcast([P, fox_w(t)]),
                                                       ALU.mult)
                    last.then_inc(a.norm_done, 1)
                else:
                    sc = score[sl][:, :].rearrange("p (g w) -> p g w", g=GQ)
                    nc.gpsimd.tensor_tensor(sc, sc, inv_l[sl][:, :].unsqueeze(2).to_broadcast([P, GQ, 2 * P]),
                                            ALU.mult).then_inc(a.norm_done, 1)

            def pair_norms(a, pi, last):
                for i in range(2 * a.steps):
                    if ahead := a_step(a, pi, i + 2, last):
                        norm_probs(a, *ahead)

            def attention(a):
                norm_probs(a, 0, 0, 0)
                norm_probs(a, 0, 0, 1)
                pair_norms(a, 0, False)
                if a.fox:
                    with pool.Fori(1, a.units // 2 - 1) as pi:
                        pair_norms(a, pi, False)
                pair_norms(a, a.units // 2 - 1, True)

            def sum_squares(c0, k):
                def pair(i, first):
                    for p in range(2):
                        for h in range(2):
                            n = 16 * k + 4 * i + 2 * p + h
                            pool.wait_ge(sq_done, n + 1)
                            wait(pool, sq_used, n)
                            if first and p == 0:
                                nc.gpsimd.tensor_copy(ssq[:, half(h)], sq[h][:, :]).then_inc(sq_used, 1)
                            else:
                                nc.gpsimd.tensor_tensor(ssq[:, half(h)], ssq[:, half(h)], sq[h][:, :], ALU.add)\
                                    .then_inc(sq_used, 1)
                pair(0, True)
                with pool.Fori(1, KD // 2) as i:
                    pair(i, False)

            def rope_cosine(c):
                pool.wait_ge(evac_done, 2 * c + 2)
                wait(pool, c_ready, c)
                nc.gpsimd.tensor_tensor(rope_part[:, :], work_a[:, :], rope_cos[:, :], ALU.mult).then_inc(cos_done, 1)
            pool.wait_ge(rope_in, 32)
            rope_cosine(0)
            with pool.Fori(1, SWA_IN - 2) as c:
                rope_cosine(c)
            attention(swa)
            sum_squares(C_O0, 0)
            sum_squares(0, 1)
            attention(fox)
            sum_squares(0, 2)
            sum_squares(0, 3)

        @block.scalar
        def _(act):
            def high(c, p):
                act.wait_ge(w_loaded[p], 8 * (c - p) + 16)
                wait(act, mm_done, 2 * c - 2)
                nc.scalar.activation(w_hi[p][:, :, :], w_raw[p][:, :, :], ACT.Copy).then_inc(w_high, 1)

            def norm_root(k):
                act.wait_ge(nat_done, k + 1)
                nc.scalar.activation(nat_y[:, :], bank[5][:, 0:TT], ACT.Sqrt, bias=eps_c[:, :], scale=1.0 / D)\
                    .then_inc(sd_done, 1)

            def norm_spread(k):
                for h in range(2):
                    act.wait_ge(bc_done, 2 * k + h + 1)
                    nc.scalar.activation(rstd[:, half(h)], bank[6 + h], ACT.Copy).then_inc(rstd_ready, 1)

            def part_high_out(m, p, before, scale, s, value, dst, row):
                act.wait_ge(s, value)
                wait(act, stored[p], 16 * (before - p))
                nc.scalar.activation(part_hi[p][:, :], work_c[:, :], ACT.Copy, scale=scale).then_inc(part_high, 1)
                act.wait_ge(part_low, before + 1)
                for t, d in ((part_hi, dst[0]), (part_lo, dst[1])):
                    act.dma_start(d[bass.ds(row * P, P), :], t[p][:, :].bitcast(FP32)).then_inc(stored[p], 16)

            def value_high_out(m, p, before, t_before, dst):
                act.wait_ge(stored[p], 16 * (before - p))
                for h in range(2):
                    act.wait_ge(part_t, 2 * t_before + h + 1)
                    nc.scalar.activation(part_hi[p][:, half(h)], bank[4 + h], ACT.Copy).then_inc(value_high, 1)
                act.wait_ge(part_low, before + 1)
                for t, d in ((part_hi, dst[0]), (part_lo, dst[1])):
                    act.dma_start(d[bass.ds(m, 1)].rearrange("a p t d -> (a p) (t d)"), t[p][:, :].bitcast(FP32))\
                        .then_inc(stored[p], 16)

            def exps(a, u, e, s):
                n = a.count(u, s)
                sl = a.ring(e, s)
                act.wait_ge(a.max_done, n + 1)
                if a.fox:
                    for i, t in enumerate(a.tiles[s]):
                        sc = score[sl][:, fox_at(t):fox_at(t) + fox_w(t)]
                        last = nc.scalar.activation(sc, sc, ACT.Exp, bias=neg_max[sl][:, i:i + 1], scale=-1.0,
                                                    accum_out=psum_l[sl][:, i:i + 1])
                    last.then_inc(a.exp_done, 1)
                    return
                for g in range(GQ):
                    w0 = 0 if s else P
                    sc = score[sl][:, g * 2 * P + w0:(g + 1) * 2 * P]
                    nc.scalar.activation(sc, sc, ACT.Exp, bias=neg_max[sl][:, g:g + 1], scale=-1.0,
                                         accum_out=psum_l[sl][:, g:g + 1])
                nc.scalar.activation(sink_e[sl][:, :], sink_e[sl][:, :], ACT.Exp).then_inc(a.exp_done, 1)

            def probs_high(a, u, e, s):
                g = a.group(s)
                par = g % 2
                wait(act, a.pv_done, a.groups * u + g - 1)
                for j, blocks in enumerate(a.blocks[s]):
                    f = a.fill(u, s) + j
                    tb = a.bank_of(u, e, s, j)[0]
                    act.wait_ge(a.t_done, f + 1)
                    if a.fox:
                        for dst, src in fox_pieces(blocks, tb, fox_p_hi[par]):
                            last = nc.scalar.activation(dst, src, ACT.Copy)
                        last.then_inc(a.ph_done, 1)
                    else:
                        nc.scalar.activation(swa_p_hi[par][:, j, :], tb, ACT.Copy).then_inc(a.ph_done, 1)

            def result_high(a, u, e, s, pi):
                g = a.group(s)
                pb = bank[O_BANK]
                act.wait_ge(a.pv_done, a.groups * u + g + 1)
                if a.fox:
                    apart(act)
                    nc.scalar.activation(o_hi[rows(e), bass.ds(pi, 1), 2 * P * g:2 * P * (g + 1)],
                                         pb[rows(e), 0:2 * P].unsqueeze(1), ACT.Copy).then_inc(a.oh_done, 1)
                else:
                    for r in range(2):
                        last = nc.scalar.activation(
                            o_hi[rows(r), 2 * u:2 * u + 2, s * P:(s + 1) * P],
                            pb.rearrange("p (a b q) -> p a b q", a=2, b=2)[rows(r), :, r, :], ACT.Copy)
                    last.then_inc(a.oh_done, 1)

            def pair_act(a, pi, first, last):
                for i in range(2 * a.steps):
                    u, e, s = a_step(a, pi, i, last)
                    probs_high(a, u, e, s)
                    if ahead := a_step(a, pi, i + 2, last):
                        exps(a, *ahead)
                    if done := a_done(a, pi, i, first):
                        result_high(a, *done)
                if last:
                    result_high(a, 2 * pi + 1, 1, a.steps - 1, pi)

            def attention(a):
                exps(a, 0, 0, 0)
                exps(a, 0, 0, 1)
                pair_act(a, 0, True, False)
                if a.fox:
                    with act.Fori(1, a.units // 2 - 1) as pi:
                        pair_act(a, pi, False, False)
                pair_act(a, a.units // 2 - 1, False, True)

            def update(c0, k, store=False, final=False):
                def pair(i, ahead=True):
                    for p in range(2):
                        c = c0 + 2 * i + p
                        m = 2 * i + p
                        for h in range(2):
                            n = 16 * k + 4 * i + 2 * p + h
                            act.wait_ge(evac_done, 2 * c + h + 1)
                            apart(act)
                            xs = x_t[:, bass.ds(m, 1), half(h)]
                            dst = (x_fin if final else h_hi)[:, bass.ds(m, 1), half(h)]
                            nc.scalar.activation(dst, xs, ACT.Copy, scale=gains[:, k + 1, bass.ds(m, 1)])\
                                .then_inc(hi_done, 1)
                            wait(act, sq_used, n - 1)
                            apart(act)
                            nc.scalar.activation(sq[h][:, :].unsqueeze(1), xs, ACT.Square).then_inc(sq_done, 1)
                        if store:
                            act.dma_start(x_scr[:, bass.ds(m, 1), :], x_t[:, bass.ds(m, 1), :]).then_inc(x_stored, 16)
                        if ahead:
                            high(c + 2, p)
                pair(0)
                if final:
                    with act.Fori(1, KD // 2 - 1) as i:
                        pair(i)
                    pair(KD // 2 - 1, False)
                else:
                    with act.Fori(1, KD // 2) as i:
                        pair(i)

            def ffn(layer, c0, k):
                for gi, (cg, cd, t0, n) in enumerate(ff_phases(c0)):
                    def pair(j):
                        tile = FT * layer + t0 + j
                        for h in range(2):
                            act.wait_ge(evac_done, 2 * (cg + 2 * j) + h + 1)
                            nc.scalar.activation(work_a[:, half(h)], work_a[:, half(h)], ACT.Silu)\
                                .then_inc(silu_done, 1)
                        high(cg + 2 * j + 2, 0)
                        for h in range(2):
                            act.wait_ge(prod_done, 2 * tile + h + 1)
                            apart(act)
                            nc.scalar.activation(hid_hi[:, bass.ds(j, 1), half(h)], work_b[:, half(h)].unsqueeze(1),
                                                 ACT.Copy).then_inc(hid_hi_done, 1)
                        high(cg + 2 * j + 3, 1)
                    if gi == 0:
                        norm_root(k)
                        norm_spread(k)
                        pair(0)
                        with act.Fori(1, n) as j:
                            pair(j)
                    else:
                        with act.Fori(0, n) as j:
                            pair(j)
                    if gi < len(FF_GROUPS) - 1:
                        with act.Fori(0, KD // 2) as i:
                            for p in range(2):
                                high(cd + 2 * i + p + 2, p)

            act.dma_start(band[:, :, :], masks[:, P:3 * P].rearrange("p (a b) -> p a b", a=2)).then_inc(const_in, 16)
            act.dma_start(causal[:, :], masks[:, 3 * P:4 * P]).then_inc(const_in, 16)
            act.dma_start(gains[:, 1:2, :], norm_ffn[0:1].rearrange("a (k p) -> p a k", p=P), allow_slow_non_contiguous=True).then_inc(const_in, 16)
            act.dma_start(gains[:, 2:3, :], norm_mix[1:2].rearrange("a (k p) -> p a k", p=P), allow_slow_non_contiguous=True).then_inc(const_in, 16)
            act.dma_start(gains[:, 3:4, :], norm_ffn[1:2].rearrange("a (k p) -> p a k", p=P), allow_slow_non_contiguous=True).then_inc(const_in, 16)
            act.dma_start(gains[:, 4:5, :], norm_final.rearrange("(a k p) -> p a k", a=1, p=P), allow_slow_non_contiguous=True).then_inc(const_in, 16)
            act.dma_start(sinks[:, :], swa_sinks.to_broadcast([P, SWA_Q])).then_inc(const_in, 16)
            for t in range(TT):
                ps = psum[:, t % 2 * D:(t % 2 + 1) * D].rearrange("p (k q) -> p k q", q=P)
                act.wait_ge(xin_t, t + 1)
                nc.scalar.activation(x_t[:, :, t * P:(t + 1) * P], ps, ACT.Copy).then_inc(start_copy, 1)
                act.wait_ge(start_copy, 2 * t + 1)
                wait(act, start_sum, t)
                nc.scalar.activation(start_sq[:, :, :], x_t[:, :, t * P:(t + 1) * P], ACT.Square)\
                    .then_inc(start_copy, 1)
                act.wait_ge(start_gain, t + 1)
                nc.scalar.activation(h_hi[:, :, t * P:(t + 1) * P],
                                     work_c[:, :].rearrange("p (k q) -> p k q", q=P), ACT.Copy).then_inc(start_hi, 1)
            high(0, 0)
            high(1, 1)
            act.wait_ge(start_copy, 2 * TT)
            act.dma_start(x_scr[:, :, :], x_t[:, :, :]).then_inc(x_stored, 16)
            norm_root(0)
            norm_spread(0)

            def swa_rope_pair(i, scale):
                for p in range(2):
                    c = 2 * i + p
                    high(c + 2, p)
                    part_high_out(c, p, c, scale, c_ready, c + 1, swa_qk, c)
            swa_rope_pair(0, -1.0)
            with act.Fori(1, 4) as i:
                swa_rope_pair(i, -1.0)
            swa_rope_pair(4, 1.0)
            for p in range(2):
                high(12 + p, p)
                value_high_out(p, p, 10 + p, p, swa_v)
            act.wait_ge(x_stored, 16)
            attention(swa)
            update(C_O0, 0)
            ffn(0, C_F0, 1)
            update(ff_phases(C_F0)[-1][1], 1, store=True)
            norm_root(2)
            norm_spread(2)
            act.wait_ge(gate_in, 32)
            nc.scalar.activation(wf_hi[:, :, :], wf_raw[:, :, :], ACT.Copy).then_inc(gate_w, 1)

            def fox_in_pair(i, scale):
                for p in range(2):
                    m = 2 * i + p
                    c = C_A1 + m
                    high(c + 2, p)
                    part_high_out(m, p, SWA_IN + m, scale, evac_done, 2 * c + 2, fox_qk, m)
            fox_in_pair(0, -1.0)
            act.wait_ge(gate_v, 4)
            nc.scalar.activation(gate[3][:, :], gate[2][:, :], ACT.Exp).then_inc(gate_a, 1)
            act.wait_ge(gate_v, 5)
            nc.scalar.activation(gate[5][:, :], gate[4][:, :], ACT.Ln).then_inc(gate_a, 1)
            with act.Fori(1, 4) as i:
                fox_in_pair(i, -1.0)
            act.wait_ge(gate_v, GATE_STEPS)
            act.dma_start(cum_scr[:, :], gate[7][:, :]).then_inc(gate_stored, 16)
            with act.Fori(4, 8) as i:
                fox_in_pair(i, 1.0)
            with act.Fori(0, 4) as i:
                for p in range(2):
                    m = 2 * i + p
                    high(C_A1 + 16 + m + 2, p)
                    value_high_out(m, p, SWA_IN + 16 + m, 2 + m, fox_v)
            act.wait_ge(x_stored, 16 * (KD + 1))
            attention(fox)
            update(C_O1, 2)
            ffn(1, C_F1, 3)
            update(ff_phases(C_F1)[-1][1], 3, final=True)
            norm_root(4)
            for t in range(TT):
                act.wait_ge(out_ready, t + 1)
                act.dma_start(out_view[t], out_tile[t % 2][:, :]).then_inc(out_stored[t % 2], 16)

        @block.vector
        def _(dve):
            V = nc.vector

            def low(c, p):
                dve.wait_ge(w_high, c + 1)
                V.tensor_tensor(w_lo[p][:, :, :], w_raw[p][:, :, :], w_hi[p][:, :, :].bitcast(FP32), ALU.subtract)\
                    .then_inc(w_split, 1)

            newton_at = [0]

            def step(ins):
                newton_at[0] += 1
                ins.then_inc(newton, 1)
                dve.wait_ge(newton, newton_at[0])

            def norm_factor(k):
                dve.wait_ge(sd_done, k + 1)
                step(V.tensor_scalar(nat_v[:, :], bank[5][:, 0:TT], 1.0 / D, EPS, ALU.mult, ALU.add))
                step(V.reciprocal(nat_y[:, :], nat_y[:, :]))
                step(V.tensor_tensor(nat_t[:, :], nat_y[:, :], nat_y[:, :], ALU.mult))
                step(V.tensor_tensor(nat_t[:, :], nat_t[:, :], nat_v[:, :], ALU.mult))
                step(V.tensor_scalar(nat_t[:, :], nat_t[:, :], -0.5, 1.5, ALU.mult, ALU.add))
                step(V.tensor_tensor(nat_y[:, :], nat_y[:, :], nat_t[:, :], ALU.mult))

            def norm_diag(k):
                norm_factor(k)
                V.tensor_tensor(diag[:, :, :], ident[:, :].unsqueeze(1).to_broadcast([P, TT, P]),
                                nat_y[:, :].unsqueeze(2).to_broadcast([P, TT, P]), ALU.mult).then_inc(diag_done, 1)

            def scale_half(c, h, dst, src):
                dve.wait_ge(mm_done, 2 * c + h + 1)
                V.tensor_tensor(dst[:, half(h)], src, rstd[:, half(h)], ALU.mult).then_inc(evac_done, 1)

            def part_low_of(p, n, scale):
                dve.wait_ge(part_high, n + 1)
                V.scalar_tensor_tensor(out=part_lo[p][:, :], in0=work_c[:, :], scalar=scale,
                                       in1=part_hi[p][:, :].bitcast(FP32), op0=ALU.mult, op1=ALU.subtract)\
                    .then_inc(part_low, 1)

            def value_strip(c, p, before, t_before):
                dve.wait_ge(part_low, before)
                for h in range(2):
                    scale_half(c, h, work_c, bank[2 * p + h])
                low(c + 2, p)
                for h in range(2):
                    dve.wait_ge(value_high, 2 * t_before + h + 1)
                    last = V.tensor_tensor(part_lo[p][:, half(h)], bank[4 + h], part_hi[p][:, half(h)].bitcast(FP32),
                                           ALU.subtract)
                last.then_inc(part_low, 1)

            def scores(a, u, e, s):
                n = a.count(u, s)
                sl = a.ring(e, s)
                ps = psum[:, s % 2 * SEQ:(s % 2 + 1) * SEQ]
                dve.wait_ge(a.qk_done, n + 1)
                if a.fox:
                    if s == 0:
                        dve.wait_ge(cum_in[e], 8 * (u - e) + 16)
                    apart(dve)
                    for i, t in enumerate(a.tiles[s]):
                        here = slice(fox_at(t), fox_at(t) + fox_w(t))
                        last = V.tensor_tensor_reduce(out=score[sl][:, here], in0=ps[:, here],
                                                      in1=cum_all[e][:, 0:fox_w(t)],
                                                      scale=SCALE, scalar=3.0e38, op0=ALU.add, op1=ALU.min,
                                                      accum_out=neg_max[sl][:, i:i + 1])
                    last.then_inc(a.max_done, 1)
                    return
                if s == 0:
                    V.memset(score[sl][:, :].rearrange("p (g w) -> p g w", g=GQ)[:, :, 0:P], 0.0)
                w0 = 0 if s else P
                for g in range(GQ):
                    at0 = g % 2 * HALF + g // 2 * 2 * P
                    V.tensor_tensor_reduce(out=score[sl][:, g * 2 * P + w0:(g + 1) * 2 * P],
                                           in0=ps[:, at0 + w0:at0 + 2 * P],
                                           in1=band[:, :, :].rearrange("p a b -> p (a b)")[:, w0:2 * P],
                                           scale=SCALE, scalar=sinks[:, GQ * u + g:GQ * u + g + 1],
                                           op0=ALU.add, op1=ALU.min,
                                           accum_out=neg_max[sl][:, g:g + 1]).then_inc(swa_row, 1)
                dve.wait_ge(swa_row, GQ * (n + 1))
                V.tensor_tensor(sink_e[sl][:, :], neg_max[sl][:, :], sinks[:, GQ * u:GQ * (u + 1)], ALU.subtract)\
                    .then_inc(a.max_done, 1)

            def inverse(a, u, e, s):
                n = a.count(u, s)
                sl = a.ring(e, s)
                dve.wait_ge(a.exp_done, n + 1)
                if a.fox:
                    m = len(a.tiles[s])
                    V.reciprocal(inv_l[sl][:, 0:m], psum_l[sl][:, 0:m]).then_inc(a.inv_done, 1)
                else:
                    V.tensor_tensor(psum_l[sl][:, :], psum_l[sl][:, :], sink_e[sl][:, :], ALU.add)\
                        .then_inc(a.sum_done, 1)
                    dve.wait_ge(a.sum_done, n + 1)
                    V.reciprocal(inv_l[sl][:, :], psum_l[sl][:, :]).then_inc(a.inv_done, 1)

            def probs_low(a, u, e, s):
                par = a.group(s) % 2
                for j, blocks in enumerate(a.blocks[s]):
                    f = a.fill(u, s) + j
                    tb = a.bank_of(u, e, s, j)[0]
                    dve.wait_ge(a.ph_done, f + 1)
                    if a.fox:
                        for (dst, src), (high_part, _) in zip(fox_pieces(blocks, tb, fox_p_lo[par]),
                                                              fox_pieces(blocks, tb, fox_p_hi[par])):
                            last = V.tensor_tensor(dst, src, high_part.bitcast(FP32), ALU.subtract)
                        last.then_inc(a.t_free, 1)
                    else:
                        V.tensor_tensor(swa_p_lo[par][:, j, :], tb, swa_p_hi[par][:, j, :].bitcast(FP32),
                                        ALU.subtract).then_inc(a.t_free, 1)

            def result_low(a, u, e, s, pi):
                g = a.group(s)
                pb = bank[O_BANK]
                dve.wait_ge(a.oh_done, a.groups * u + g + 1)
                if a.fox:
                    at0 = (rows(e), bass.ds(pi, 1), slice(2 * P * g, 2 * P * (g + 1)))
                    V.tensor_tensor(o_lo[at0], pb[rows(e), 0:2 * P].unsqueeze(1), o_hi[at0].bitcast(FP32),
                                    ALU.subtract).then_inc(a.o_free, 1)
                else:
                    for r in range(2):
                        at0 = (rows(r), slice(2 * u, 2 * u + 2), slice(s * P, (s + 1) * P))
                        last = V.tensor_tensor(o_lo[at0],
                                               pb.rearrange("p (a b q) -> p a b q", a=2, b=2)[rows(r), :, r, :],
                                               o_hi[at0].bitcast(FP32), ALU.subtract)
                    last.then_inc(a.o_free, 1)

            def pair_dve(a, pi, first, last):
                for i in range(2 * a.steps):
                    u, e, s = a_step(a, pi, i, last)
                    probs_low(a, u, e, s)
                    if ahead := a_step(a, pi, i + 3, last):
                        scores(a, *ahead)
                    if ahead := a_step(a, pi, i + 2, last):
                        inverse(a, *ahead)
                    if done := a_done(a, pi, i, first):
                        result_low(a, *done)
                if last:
                    result_low(a, 2 * pi + 1, 1, a.steps - 1, pi)

            def attention(a):
                scores(a, 0, 0, 0)
                scores(a, 0, 0, 1)
                inverse(a, 0, 0, 0)
                scores(a, 0, 0, 2)
                inverse(a, 0, 0, 1)
                pair_dve(a, 0, True, False)
                if a.fox:
                    with dve.Fori(1, a.units // 2 - 1) as pi:
                        pair_dve(a, pi, False, False)
                pair_dve(a, a.units // 2 - 1, False, True)

            def update(c0, k, back=None, ahead_last=True, final=False, plain=False):
                def pair(i, ahead=True, back_sem=None):
                    if back_sem is not None:
                        dve.wait_ge(back_sem, 16)
                    for p in range(2):
                        c = c0 + 2 * i + p
                        m = 2 * i + p
                        for h in range(2):
                            dve.wait_ge(mm_done, 2 * c + h + 1)
                            xs = x_t[:, bass.ds(m, 1), half(h)]
                            V.tensor_tensor(xs, bank[2 * p + h].unsqueeze(1), xs, ALU.add).then_inc(evac_done, 1)
                        if not (plain or final):
                            for h in range(2):
                                n = 16 * k + 4 * i + 2 * p + h
                                dve.wait_ge(hi_done, n + 1)
                                xs = x_t[:, bass.ds(m, 1), half(h)]
                                V.scalar_tensor_tensor(out=h_lo[:, bass.ds(m, 1), half(h)], in0=xs,
                                                       scalar=gains[:, k + 1, bass.ds(m, 1)],
                                                       in1=h_hi[:, bass.ds(m, 1), half(h)].bitcast(FP32),
                                                       op0=ALU.mult, op1=ALU.subtract).then_inc(h_ready, 1)
                        if ahead:
                            low(c + 2, p)
                pair(0, back_sem=x_back[back] if back is not None else None)
                if back is not None:
                    dve.wait_ge(x_back[back + 1], 16)
                if final:
                    with dve.Fori(1, KD // 2 - 1) as i:
                        pair(i)
                    pair(KD // 2 - 1, False)
                else:
                    with dve.Fori(1, KD // 2) as i:
                        pair(i)

            def ffn(layer, c0, k):
                for gi, (cg, cd, t0, n) in enumerate(ff_phases(c0)):
                    def pair(j):
                        tile = FT * layer + t0 + j
                        c = cg + 2 * j
                        if not (isinstance(tile, int) and tile == 0):
                            dve.wait_ge(prod_done, 2 * tile)
                        for h in range(2):
                            scale_half(c, h, work_a, bank[h])
                        low(c + 2, 0)
                        if not (isinstance(tile, int) and tile == 0):
                            dve.wait_ge(hid_ready, 2 * tile)
                        for h in range(2):
                            scale_half(c + 1, h, work_b, bank[2 + h])
                        for h in range(2):
                            dve.wait_ge(silu_done, 2 * tile + h + 1)
                            dve.wait_ge(evac_done, 2 * (c + 1) + h + 1)
                            V.tensor_tensor(work_b[:, half(h)], work_b[:, half(h)], work_a[:, half(h)], ALU.mult)\
                                .then_inc(prod_done, 1)
                        for h in range(2):
                            dve.wait_ge(hid_hi_done, 2 * tile + h + 1)
                            V.tensor_tensor(hid_lo[:, bass.ds(j, 1), half(h)], work_b[:, half(h)].unsqueeze(1),
                                            hid_hi[:, bass.ds(j, 1), half(h)].bitcast(FP32), ALU.subtract)\
                                .then_inc(hid_ready, 1)
                        low(c + 3, 1)
                    if gi == 0:
                        norm_diag(k)
                        dve.wait_ge(rstd_ready, 2 * k + 2)
                        pair(0)
                        with dve.Fori(1, n) as j:
                            pair(j)
                    else:
                        with dve.Fori(0, n) as j:
                            pair(j)
                    if gi < len(FF_GROUPS) - 1:
                        update(cd, None, plain=True)

            V.memset(eps_c[:, :], EPS)
            dve.wait_ge(const_in, 16 * N_CONST)
            V.tensor_copy(ident_bf[:, :], ident[:, :]).then_inc(const_ready, 1)
            V.tensor_copy(causal_bf[:, :], causal[:, :]).then_inc(const_ready, 1)
            V.tensor_scalar(sinks[:, :], sinks[:, :], -1.0, None, ALU.mult).then_inc(const_ready, 1)
            for t in range(TT):
                wc = work_c[:, :].rearrange("p (k q) -> p k q", q=P)
                dve.wait_ge(start_copy, 2 * t + 1)
                wait(dve, h_ready, t)
                V.tensor_tensor(wc, x_t[:, :, t * P:(t + 1) * P], gains[:, 0, :].unsqueeze(2).to_broadcast([P, KD, P]), ALU.mult)\
                    .then_inc(start_gain, 1)
                dve.wait_ge(start_copy, 2 * t + 2)
                V.tensor_reduce(ssq[:, t * P:(t + 1) * P], start_sq[:, :, :].rearrange("p k q -> p q k"),
                                AX.X, ALU.add).then_inc(start_sum, 1)
                dve.wait_ge(start_hi, t + 1)
                V.tensor_tensor(h_lo[:, :, t * P:(t + 1) * P], wc,
                                h_hi[:, :, t * P:(t + 1) * P].bitcast(FP32), ALU.subtract).then_inc(h_ready, 1)
            low(0, 0)
            low(1, 1)
            norm_diag(0)
            dve.wait_ge(rstd_ready, 2)

            def swa_rope_strip(c, p, first=False, before=-1.0):
                if not first:
                    dve.wait_ge(c_ready, c)
                scale_half(c, 0, work_a, bank[2 * p])
                if not first:
                    part_low_of(1 - p, c - 1, before)
                scale_half(c, 1, work_a, bank[2 * p + 1])
                low(c + 2, p)
                dve.wait_ge(evac_done, 2 * c + 2)
                for b in range(4):
                    last = V.tensor_copy(work_b[32 * b:32 * b + 32, :], work_a[32 * (b ^ 1):32 * (b ^ 1) + 32, :])
                last.then_inc(swapped, 1)
                dve.wait_ge(swapped, c + 1)
                if first:
                    dve.wait_ge(rope_in, 32)
                V.tensor_tensor(work_b[:, :], work_b[:, :], rope_sin[:, :], ALU.mult).then_inc(sin_done, 1)
                dve.wait_ge(sin_done, c + 1)
                dve.wait_ge(cos_done, c + 1)
                if not first:
                    dve.wait_ge(part_low, c)
                V.tensor_tensor(work_c[:, :], rope_part[:, :], work_b[:, :], ALU.add).then_inc(c_ready, 1)
            swa_rope_strip(0, 0, True)
            swa_rope_strip(1, 1)
            with dve.Fori(1, 4) as i:
                for p in range(2):
                    swa_rope_strip(2 * i + p, p)
            swa_rope_strip(8, 0)
            swa_rope_strip(9, 1, before=1.0)
            dve.wait_ge(c_ready, SWA_IN - 2)
            part_low_of(1, SWA_IN - 3, 1.0)
            for p in range(2):
                value_strip(10 + p, p, 10 + p, p)
            attention(swa)
            update(C_O0, 0, back=0)
            ffn(0, C_F0, 1)
            update(ff_phases(C_F0)[-1][1], 1)
            norm_diag(2)
            dve.wait_ge(rstd_ready, 6)
            dve.wait_ge(gate_w, 1)
            V.tensor_tensor(wf_lo[:, :, :], wf_raw[:, :, :], wf_hi[:, :, :].bitcast(FP32), ALU.subtract)\
                .then_inc(gate_w, 1)

            def fox_in_strip(m, p, scale=-1.0):
                dve.wait_ge(part_low, SWA_IN + m)
                for h in range(2):
                    scale_half(C_A1 + m, h, work_c, bank[2 * p + h])
                low(C_A1 + m + 2, p)
                part_low_of(p, SWA_IN - 2 + m, scale)
            fox_in_strip(0, 0)
            fox_in_strip(1, 1)
            G = [g[:, :] for g in gate]
            gate_at = [0]

            def gate_step(ins):
                gate_at[0] += 1
                ins.then_inc(gate_v, 1)
                dve.wait_ge(gate_v, gate_at[0])
            dve.wait_ge(gate_mm, 1)
            gate_step(V.tensor_tensor(G[0], psum[0:FOX_H, 4 * HALF:6 * HALF], rstd[0:FOX_H, :], ALU.mult))
            gate_step(V.tensor_scalar(G[0], G[0], f_bias[:, :], None, ALU.add))
            gate_step(V.tensor_scalar(G[1], G[0], -1.0, None, ALU.mult))
            gate_step(V.tensor_tensor(G[2], G[0], G[1], ALU.min))
            dve.wait_ge(gate_a, 1)
            gate_step(V.tensor_scalar(G[4], G[3], 1.0, None, ALU.add))
            gate_step(V.tensor_scalar(G[1], G[4], -1.0, None, ALU.add))
            gate_step(V.tensor_tensor(G[1], G[3], G[1], ALU.subtract))
            dve.wait_ge(gate_a, 2)
            gate_step(V.reciprocal(G[6], G[4]))
            gate_step(V.tensor_tensor(G[1], G[1], G[6], ALU.mult))
            gate_step(V.tensor_tensor(G[5], G[5], G[1], ALU.add))
            gate_step(V.tensor_scalar(G[0], G[0], 0.0, 1.0 / SCALE, ALU.min, ALU.mult))
            gate_step(V.scalar_tensor_tensor(out=G[5], in0=G[5], scalar=-1.0 / SCALE, in1=G[0],
                                             op0=ALU.mult, op1=ALU.add))
            gate_step(V.memset(G[2], 1.0))
            gate_step(V.tensor_tensor_scan(G[7], G[2], G[5], 0.0, ALU.mult, ALU.add))
            assert gate_at[0] == GATE_STEPS, gate_at
            with dve.Fori(1, 4) as i:
                for p in range(2):
                    fox_in_strip(2 * i + p, p)
            with dve.Fori(4, 8) as i:
                for p in range(2):
                    fox_in_strip(2 * i + p, p, 1.0)
            with dve.Fori(0, 4) as i:
                for p in range(2):
                    m = 2 * i + p
                    value_strip(C_A1 + 16 + m, p, SWA_IN + 16 + m, 2 + m)
            attention(fox)
            update(C_O1, 2, back=2)
            ffn(1, C_F1, 3)
            update(ff_phases(C_F1)[-1][1], 3, final=True)
            norm_factor(4)
            for t in range(TT):
                dve.wait_ge(out_t, t + 1)
                if t >= 2:
                    dve.wait_ge(out_stored[t % 2], 16 * (t // 2))
                V.tensor_scalar(out_tile[t % 2][:, :], psum[:, t % 2 * D:(t % 2 + 1) * D], nat_y[:, t:t + 1], None,
                                ALU.mult).then_inc(out_ready, 1)

        @block.tensor
        def _(pe):
            T = nc.tensor

            def chunk(c, p, n, mh, ml, ready=None, after=None):
                pe.wait_ge(w_split, c + 1)
                for h in range(2):
                    wait(pe, evac_done, 2 * c + h - 3)
                    for k in range(n):
                        if ready:
                            ready(h, k)
                        T.matmul(bank[2 * p + h], w_hi[p][:, k, :], mh[:, k, half(h)], start=k == 0, stop=False)
                        T.matmul(bank[2 * p + h], w_hi[p][:, k, :], ml[:, k, half(h)], start=False, stop=False)
                        last = T.matmul(bank[2 * p + h], w_lo[p][:, k, :], mh[:, k, half(h)], start=False,
                                        stop=k == n - 1)
                    last.then_inc(mm_done, 1)
                    if after:
                        after(h)

            def norm_sums(k):
                if k == 0:
                    pe.wait_ge(start_sum, TT)
                    pe.wait_ge(const_ready, 4)
                else:
                    pe.wait_ge(sq_used, 16 * k)
                for t in range(TT):
                    last = T.matmul(bank[5][:, t:t + 1], ssq[:, t * P:(t + 1) * P], ones[:, 0:1], start=True, stop=True)
                last.then_inc(nat_done, 1)

            def norm_bc(k):
                pe.wait_ge(diag_done, k_diag(k) + 1)
                for h in range(2):
                    T.matmul(bank[6 + h], ones[:, :], diag[:, 4 * h:4 * h + 4, :], start=True, stop=True)\
                        .then_inc(bc_done, 1)

            def k_diag(k):
                return k

            def linear(c0, pairs, n, mh, ml, ready=None, norm=None):
                def after0(h):
                    if norm is not None and h == 0:
                        norm_sums(norm)

                def after1(h):
                    if norm is not None and h == 0:
                        norm_bc(norm)
                chunk(c0, 0, n, mh, ml, ready, after0)
                chunk(c0 + 1, 1, n, mh, ml, None, after1)

            def values_t(c, before):
                pe.wait_ge(evac_done, 2 * c + 2)
                for h in range(2):
                    pe.wait_ge(part_low, before)
                    for b in range(4):
                        last = T.transpose(bank[4 + h][:, b * P:(b + 1) * P], work_c[:, (4 * h + b) * P:(4 * h + b + 1) * P],
                                           ident[:, :])
                    last.then_inc(part_t, 1)

            def value_chunks(c0, pairs, before):
                def pair(i, first):
                    for p in range(2):
                        c = c0 + 2 * i + p
                        n = before + 2 * i + p

                        def after(h):
                            if h == 0 and not (first and p == 0):
                                values_t(c - 1, n - 1)
                        chunk(c, p, KD, h_hi, h_lo, None, after)
                pair(0, True)
                if pairs > 1:
                    with pe.Fori(1, pairs) as i:
                        pair(i, False)
                values_t(c0 + 2 * pairs - 1, before + 2 * pairs - 1)

            def linear_rest(c0, pairs, n, mh, ml, first=1):
                with pe.Fori(first, pairs) as i:
                    for p in range(2):
                        chunk(c0 + 2 * i + p, p, n, mh, ml)

            def h_wait(base):
                def ready(h, k):
                    pe.wait_ge(h_ready, base + 2 * k + h + 1)
                return ready

            def qk(a, u, e, s):
                n = a.count(u, s)
                at0 = s % 2 * SEQ
                wait(pe, a.max_done, n - 1)
                if s == 0:
                    pe.wait_ge(a.qk_in[e], 8 * a.qk_dmas * (u - e + 2))
                if a.fox:
                    q_hi, q_lo, key = fox_operands(u, e)[:3]
                    for t in a.tiles[s]:
                        qs, w = slice(t * P, (t + 1) * P), fox_w(t)
                        for cc in range(0, w, HALF):
                            ww = min(HALF, w - cc)
                            ps = psum[:, at0 + fox_at(t) + cc:at0 + fox_at(t) + cc + ww]
                            diagonal = cc + ww == w
                            T.matmul(ps, q_hi[:, qs], key[:, cc:cc + ww], start=True, stop=False)
                            last = T.matmul(ps, q_lo[rows(0), qs], key[rows(0), cc:cc + ww], start=False,
                                            stop=not diagonal)
                            if diagonal:
                                last = T.matmul(ps[:, ww - P:ww], ident_bf[:, :], causal_bf[:, :], start=False,
                                                stop=True)
                else:
                    qs = slice(s * P, (s + 1) * P)
                    k0 = (s - 1) * P if s else 0
                    w0 = 0 if s else P
                    for pr in range(2):
                        for n3, (qq, kk) in enumerate(((swa_q_hi, swa_k_hi), (swa_q_hi, swa_k_lo),
                                                       (swa_q_lo, swa_k_hi))):
                            for r in range(2):
                                last = T.matmul(bank[s % 2 * 2 + r][:, pr * 2 * P + w0:(pr + 1) * 2 * P],
                                                qq[e][rows(r), pr, qs], kk[e][rows(r), k0:(s + 1) * P],
                                                start=n3 == 0, stop=n3 == 2)
                last.then_inc(a.qk_done, 1)

            def transposes(a, u, e, s):
                n = a.count(u, s)
                sl = a.ring(e, s)
                pe.wait_ge(a.norm_done, n + 1)
                for j, blocks in enumerate(a.blocks[s]):
                    f = a.fill(u, s) + j
                    tb, ago = a.bank_of(u, e, s, j)
                    wait(pe, a.t_free, f - ago + 1)
                    if a.fox:
                        sources = [fox_at(t) + (k + b) * P for t, k, n in blocks for b in range(n)]
                    else:
                        sources = [b * 2 * P + j * P for b in range(GQ)]
                    for b, at0 in enumerate(sources):
                        last = T.transpose(tb[:, b * P:(b + 1) * P], score[sl][:, at0:at0 + P], ident[:, :])
                    last.then_inc(a.t_done, 1)

            def pv(a, u, e, s, pi):
                g = a.group(s)
                par, t = g % 2, a.tiles[s][-1]
                pb = bank[O_BANK]
                pe.wait_ge(a.t_free, a.fill(u, s) + a.fills[s])
                wait(pe, a.o_free, a.groups * u + g)
                if g == 0:
                    pe.wait_ge(a.v_in[e], 8 * a.v_dmas * (u - e + 2))
                if a.fox:
                    terms = [(k, k, slice(0 if k < t else P, 2 * P)) for k in range(t + 1)]
                    ph, pl = fox_p_hi[par], fox_p_lo[par]
                    vh, vl = fox_operands(u, e)[3:]
                else:
                    terms = [(t - 1 + j, j, slice(0, HALF)) for j in range(0 if t else 1, 2)]
                    ph, pl, vh, vl = swa_p_hi[par], swa_p_lo[par], v_hi[e], v_lo[e]
                for i, (vt, pt, cs) in enumerate(terms):
                    T.matmul(pb[:, cs], vh[:, vt, :], ph[:, pt, cs], start=i == 0, stop=False)
                    T.matmul(pb[:, cs], vh[:, vt, :], pl[:, pt, cs], start=False, stop=False)
                    last = T.matmul(pb[:, cs], vl[:, vt, :], ph[:, pt, cs], start=False, stop=i == len(terms) - 1)
                last.then_inc(a.pv_done, 1)

            def pair_pe(a, pi, first, last):
                for i in range(2 * a.steps):
                    u, e, s = a_step(a, pi, i, last)
                    transposes(a, u, e, s)
                    if ahead := a_step(a, pi, i + 3, last):
                        qk(a, *ahead)
                    if done := a_done(a, pi, i, first):
                        pv(a, *done)
                if last:
                    pv(a, 2 * pi + 1, 1, a.steps - 1, pi)

            def attention(a):
                pe.wait_ge(evac_done, 2 * (C_O1 if a.fox else C_O0))
                pe.wait_ge(rstd_ready, 6 if a.fox else 2)
                qk(a, 0, 0, 0)
                qk(a, 0, 0, 1)
                qk(a, 0, 0, 2)
                pair_pe(a, 0, True, False)
                if a.fox:
                    with pe.Fori(1, a.units // 2 - 1) as pi:
                        pair_pe(a, pi, False, False)
                pair_pe(a, a.units // 2 - 1, False, True)

            def out_projection(a, c0):
                pe.wait_ge(a.o_free, a.groups * a.units)
                linear(c0, KD // 2, KD, o_hi, o_lo)
                linear_rest(c0, KD // 2, KD, o_hi, o_lo)

            def ffn(layer, c0, h_base, k):
                for gi, (cg, cd, t0, n) in enumerate(ff_phases(c0)):
                    if gi == 0:
                        linear(cg, n, KD, h_hi, h_lo, h_wait(h_base), norm=k)
                        linear_rest(cg, n, KD, h_hi, h_lo)
                    else:
                        linear_rest(cg, n, KD, h_hi, h_lo, first=0)

                    def hid_wait(h, kk, t0=t0):
                        pe.wait_ge(hid_ready, 2 * (FT * layer + t0 + kk) + h + 1)
                    linear(cd, KD // 2, n, hid_hi, hid_lo, hid_wait)
                    linear_rest(cd, KD // 2, n, hid_hi, hid_lo)

            pe.wait_ge(const_in, 16 * N_CONST)
            for t in range(TT):
                pe.wait_ge(xin_loaded[t % 2], 16 * (t // 2 + 1))
                if t >= 2:
                    pe.wait_ge(start_copy, 2 * (t - 2) + 1)
                for k in range(KD):
                    at0 = t % 2 * D + k * P
                    last = T.transpose(psum[:, at0:at0 + P], start_x[t % 2][:, k * P:(k + 1) * P], ident[:, :])
                last.then_inc(xin_t, 1)
            pe.wait_ge(start_copy, 2 * TT - 1)

            def start_wait(h, k):
                if k == 0:
                    pe.wait_ge(h_ready, 4 * h + 4)
            linear(C_A0, SWA_IN // 2, KD, h_hi, h_lo, start_wait, norm=0)
            linear_rest(C_A0, 5, KD, h_hi, h_lo)
            value_chunks(C_A0 + 10, 1, SWA_IN - 2)
            attention(swa)
            out_projection(swa, C_O0)
            ffn(0, C_F0, TT, 1)
            linear(C_A1, FOX_IN // 2, KD, h_hi, h_lo, h_wait(TT + 2 * KD), norm=2)
            pe.wait_ge(gate_w, 2)
            for h in range(2):
                for k in range(KD):
                    dst = bank[4 + h][0:FOX_H, :]
                    T.matmul(dst, wf_hi[:, k, :], h_hi[:, k, half(h)], start=k == 0, stop=False)
                    T.matmul(dst, wf_hi[:, k, :], h_lo[:, k, half(h)], start=False, stop=False)
                    last = T.matmul(dst, wf_lo[:, k, :], h_hi[:, k, half(h)], start=False, stop=k == KD - 1)
            last.then_inc(gate_mm, 1)
            linear_rest(C_A1, 8, KD, h_hi, h_lo)
            value_chunks(C_A1 + 16, 4, SWA_IN + 16)
            attention(fox)
            out_projection(fox, C_O1)
            ffn(1, C_F1, TT + 4 * KD, 3)
            norm_sums(4)
            pe.wait_ge(hi_done, 64)
            pe.wait_ge(evac_done, 2 * C_END)
            for t in range(TT):
                if t >= 2:
                    pe.wait_ge(out_ready, t - 1)
                for k in range(KD):
                    at0 = t % 2 * D + k * P
                    last = T.transpose(psum[:, at0:at0 + P], x_fin[:, k, t * P:(t + 1) * P], ident[:, :])
                last.then_inc(out_t, 1)


_INS = ["x", "norm_mix", "norm_ffn", "swa_w_in", "swa_sinks", "swa_w_out", "fox_w_in", "fox_f_bias", "fox_w_out",
        "ffn_w_gate_up", "ffn_w_down", "norm_final"]


def _constants():
    half_d = HD // 2
    inv_freq = (10000.0 ** (-np.arange(half_d, dtype=np.float64) / half_d)).astype(np.float32)
    ang = (np.arange(SEQ, dtype=np.float32)[None, :] * inv_freq[:, None]).astype(np.float64)
    cos, sin = np.cos(ang), np.sin(ang)
    rope = np.stack([np.concatenate([cos] * 4), np.concatenate([-sin, sin] * 2)]).astype(np.float32)
    q, k = np.arange(P)[:, None], np.arange(P)[None, :]
    previous = np.where(k // CHUNK >= q // CHUNK + 1, 0.0, BIG)
    own = np.where(k // CHUNK <= q // CHUNK, 0.0, BIG)
    causal = np.where(k <= q, 0.0, BIG)
    masks = np.concatenate([np.eye(P), previous, own, causal], axis=1).astype(np.float32)
    return rope, masks


def kernel(**inputs):
    import concourse.bacc as bacc
    from concourse.bass_utils import run_bass_kernel_spmd

    nc = bacc.Bacc("TRN2", target_bir_lowering=False, num_devices=1)
    rope, masks = _constants()
    arrays, args = {}, {}
    for name in _INS:
        a = np.ascontiguousarray(inputs[name])
        arrays[f"in_{name}"] = a
        args[name] = nc.dram_tensor(f"in_{name}", a.shape, mybir.dt.from_np(a.dtype), kind="ExternalInput").ap()
    for name, a in (("rope", rope), ("masks", masks)):
        arrays[f"in_{name}"] = a
        args[name] = nc.dram_tensor(f"in_{name}", a.shape, FP32, kind="ExternalInput").ap()
    out = nc.dram_tensor("out_0", (1, SEQ, D), FP32, kind="ExternalOutput").ap()
    trunk(nc, args["x"], args["norm_mix"], args["norm_ffn"], args["swa_w_in"], args["swa_sinks"],
          args["swa_w_out"], args["fox_w_in"], args["fox_f_bias"], args["fox_w_out"], args["ffn_w_gate_up"],
          args["ffn_w_down"], args["norm_final"], args["rope"], args["masks"], out)
    r = run_bass_kernel_spmd(nc, [arrays], core_ids=[0])
    return r.results[0]["out_0"]
```

```python
import numpy as np
from contextlib import ExitStack

import concourse.bass as bass
from concourse import mybir

FP32 = mybir.dt.float32
F32R = mybir.dt.float32r
BF16 = mybir.dt.bfloat16
ALU = mybir.AluOpType
ACT = mybir.ActivationFunctionType
AX = mybir.AxisListType

P = 128
SEQ = 1024
D = 1024
KD = D // P
TT = SEQ // P
HALF = SEQ // 2
HD = 64
CHUNK = 64
SWA_Q, SWA_KV = 16, 4
GQ = SWA_Q // SWA_KV
FOX_H = 16
D_FF = 2816
FT = D_FF // P
FF_GROUPS = (8, 7, 7)
SWA_IN = (SWA_Q + 2 * SWA_KV) * HD // P
FOX_IN = 3 * FOX_H * HD // P
EPS = 1e-6
SCALE = HD ** -0.5
BIG = 1e30


def trunk(nc, x, norm_mix, norm_ffn, swa_w_in, swa_sinks, swa_w_out, fox_w_in, fox_f_bias, fox_w_out,
          w_gate_up, w_down, norm_final, rope, masks, out):
    ctx = ExitStack()
    with ctx:
        base = (nc.sbuf_base + 63) // 64 * 64

        def at(name, kib, shape, dt=FP32):
            return nc.alloc_sbuf_tensor_at(name, shape, dt, offset=base + int(kib * 1024))

        x_t = at("x_t", 0, [P, KD, SEQ])
        fox_p_hi = [at(f"fox_p_hi{i}", 16 * i, [P, TT, 2 * P], F32R) for i in range(2)]
        fox_p_lo = [at(f"fox_p_lo{i}", 16 * i + 8, [P, TT, 2 * P], F32R) for i in range(2)]
        swa_p_hi = [at(f"swa_p_hi{i}", 8 * i, [P, 2, GQ * P], F32R) for i in range(2)]
        swa_p_lo = [at(f"swa_p_lo{i}", 8 * i + 4, [P, 2, GQ * P], F32R) for i in range(2)]
        h_hi = at("h_hi", 32, [P, KD, SEQ], F32R)
        h_lo = at("h_lo", 64, [P, KD, SEQ], F32R)
        x_fin = at("x_fin", 32, [P, KD, SEQ])
        score = [at(f"score{i}", (32, 36, 40, 44, 88, 92)[i], [P, SEQ]) for i in range(6)]
        fox_values = [at(f"fox_values{i}", 48 + 4 * i, [P, TT, P], F32R) for i in range(2)]
        v_low_part = [at(f"v_low_part{i}", 56 + i, [P, 2 * P]) for i in range(2)]
        joint = [at(f"joint{i}", 58 + i, [P, 2 * P]) for i in range(2)]
        v_hi = [at(f"v_hi{i}", 48 + 8 * i, [P, TT, P], F32R) for i in range(2)]
        v_lo = [at(f"v_lo{i}", 52 + 8 * i, [P, TT, P], F32R) for i in range(2)]
        fox_q_hi = [at(f"fox_q_hi{i}", 64 + 12 * i, [P, SEQ], F32R) for i in range(2)]
        fox_q_lo = [at(f"fox_q_lo{i}", 68 + 12 * i, [P, SEQ], F32R) for i in range(2)]
        fox_k = [at(f"fox_k{i}", 72 + 12 * i, [P, SEQ], F32R) for i in range(2)]
        fox_first = [at("fox_first_q_hi", 112, [P, SEQ], F32R), at("fox_first_q_lo", 116, [P, SEQ], F32R),
                     at("fox_first_k", 120, [P, SEQ], F32R), at("fox_first_v", 124, [P, TT, P], F32R)]
        swa_q = [at("swa_q0", 16, [P, GQ, SEQ], F32R), at("swa_q1", 64, [P, GQ, SEQ], F32R)]
        swa_k_hi = [at("swa_k_hi0", 152, [P, SEQ], F32R), at("swa_k_hi1", 80, [P, SEQ], F32R)]
        swa_k_lo = [at("swa_k_lo0", 156, [P, SEQ], F32R), at("swa_k_lo1", 84, [P, SEQ], F32R)]
        o_hi = at("o_hi", 96, [P, KD, SEQ], F32R)
        o_lo = at("o_lo", 128, [P, KD, SEQ], F32R)
        hid_hi = at("hid_hi", 96, [P, 8, SEQ], F32R)
        hid_lo = at("hid_lo", 128, [P, 8, SEQ], F32R)
        rope_cos = at("rope_cos", 96, [P, SEQ])
        rope_sin = at("rope_sin", 100, [P, SEQ])
        rope_part = at("rope_part", 116, [P, SEQ])
        start_sq = at("start_sq", 128, [P, KD, SEQ])
        start_x = [at(f"start_x{i}", (108, 112, 120, 124)[i], [P, D]) for i in range(4)]
        gate = [at(f"gate{i}", 96 + 4 * i, [FOX_H, SEQ]) for i in range(8)]
        out_tile = [at(f"out_tile{i}", 96 + 4 * i, [P, D]) for i in range(TT)]
        w_raw = [at(f"w_raw{i}", 160 + 4 * i, [P, KD, P]) for i in range(2)]
        w_hi = [at(f"w_hi{i}", 168 + 4 * i, [P, KD, P], F32R) for i in range(2)]
        w_lo = [at(f"w_lo{i}", 176 + 4 * i, [P, KD, P], F32R) for i in range(2)]
        rstd = at("rstd", 184, [P, SEQ])
        ssq = at("ssq", 188, [P, SEQ])
        work_a = at("work_a", 192, [P, SEQ])
        work_b = at("work_b", 196, [P, SEQ])
        work_c = at("work_c", 200, [P, SEQ])
        start_h = [at(f"start_h{i}", 196 + 4 * i, [P, KD, P]) for i in range(2)]
        diag = at("diag", 196, [P, TT, P])
        sq = [at(f"sq{i}", 192 + 2 * i, [P, HALF]) for i in range(2)]
        cum_all = [at(f"cum_all{i}", 192 + 4 * i, [P, SEQ]) for i in range(2)]
        small_at = [204 * 1024]

        def small(name, shape, dt=FP32):
            size = int(np.prod(shape[1:])) * (2 if dt == BF16 else 4)
            t = nc.alloc_sbuf_tensor_at(name, shape, dt, offset=base + small_at[0], align_bytes=8)
            small_at[0] += (size + 7) // 8 * 8
            assert base + small_at[0] <= nc.sbuf_usable_end
            return t

        ident = small("ident", [P, P])
        ident_bf = small("ident_bf", [P, P], BF16)
        causal_bf = small("causal_bf", [P, P], BF16)
        band_bf = small("band_bf", [P, 2 * P], BF16)
        ones = small("ones", [P, P])
        gains = small("gains", [P, 5, KD])
        sinks = small("sinks", [P, SWA_Q])
        f_bias = small("f_bias", [FOX_H, 1])
        nat_v = small("nat_v", [P, TT])
        nat_y = small("nat_y", [P, TT])
        nat_t = small("nat_t", [P, TT])
        neg_max = [small(f"neg_max{i}", [P, GQ]) for i in range(6)]
        psum_l = [small(f"psum_l{i}", [P, GQ]) for i in range(6)]
        sink_e = [small(f"sink_e{i}", [P, GQ]) for i in range(4)]
        inv_l = [small(f"inv_l{i}", [P, GQ]) for i in range(6)]
        eps_c = small("eps_c", [P, 1])
        warm = small("warm", [P, 1])
        part_hi = [at(f"part_hi{i}", 136 + 4 * i, [P, SEQ], F32R) for i in range(2)]
        part_lo = [at(f"part_lo{i}", 144 + 4 * i, [P, SEQ], F32R) for i in range(2)]
        wf_lo = at("wf_lo", 128, [P, KD, FOX_H], F32R)
        wf_raw = at("wf_raw", 129, [P, KD, FOX_H])
        wf_hi = at("wf_hi", 130, [P, KD, FOX_H], F32R)
        causal = at("causal", 104, [P, P])
        band = at("band", 105, [P, 2 * P])

        psum = nc.alloc_psum_tensor("psum", [P, 8 * HALF], FP32)
        bank = [psum[:, i * HALF:(i + 1) * HALF] for i in range(8)]

        x_scr = nc.dram_tensor("x_scr", [P, KD, SEQ], FP32).ap()
        swa_qk = [nc.dram_tensor(f"swa_qk_{w}", [(SWA_Q + SWA_KV) * HD, SEQ], FP32).ap() for w in ("hi", "lo")]
        swa_v = [nc.dram_tensor(f"swa_v_{w}", [SWA_KV // 2 * P, TT, P], FP32).ap() for w in ("hi", "lo")]
        fox_qk = [nc.dram_tensor(f"fox_qk_{w}", [2 * FOX_H * HD, SEQ], FP32).ap() for w in ("hi", "lo")]
        fox_v = [nc.dram_tensor(f"fox_v_{w}", [FOX_H // 2 * P, TT, P], FP32).ap() for w in ("hi", "lo")]
        cum_scr = nc.dram_tensor("cum_scr", [FOX_H, SEQ], FP32).ap()

        def sem(name):
            return ctx.enter_context(nc.semaphore(name))

        w_loaded = [sem(f"w_loaded{i}") for i in range(2)]
        w_high = sem("w_high")
        w_split = sem("w_split")
        mm_done = sem("mm_done")
        evac_done = sem("evac_done")
        ident_in = sem("ident_in")
        gain_in = sem("gain_in")
        ones_ready = sem("ones_ready")
        const_in = sem("const_in")
        rope_in = sem("rope_in")
        const_ready = sem("const_ready")
        xin_loaded = [sem(f"xin_loaded{i}") for i in range(4)]
        xin_t = sem("xin_t")
        start_copy = sem("start_copy")
        start_square = sem("start_square")
        start_gain = sem("start_gain")
        start_hi = sem("start_hi")
        start_sum = sem("start_sum")
        h_ready = sem("h_ready")
        hi_done = sem("hi_done")
        sq_done = sem("sq_done")
        sq_used = sem("sq_used")
        nat_done = sem("nat_done")
        sd_done = sem("sd_done")
        newton = sem("newton")
        diag_done = sem("diag_done")
        bc_done = sem("bc_done")
        rstd_ready = sem("rstd_ready")
        swapped = sem("swapped")
        cos_done = sem("cos_done")
        sin_done = sem("sin_done")
        c_ready = sem("c_ready")
        part_high = sem("part_high")
        part_low = sem("part_low")
        value_high = sem("value_high")
        part_t = sem("part_t")
        stored = [sem(f"stored{i}") for i in range(2)]
        gate_in = sem("gate_in")
        gate_w = sem("gate_w")
        gate_mm = sem("gate_mm")
        gate_v = sem("gate_v")
        gate_a = sem("gate_a")
        gate_stored = sem("gate_stored")
        silu_done = sem("silu_done")
        prod_done = sem("prod_done")
        hid_hi_done = sem("hid_hi_done")
        hid_ready = sem("hid_ready")
        x_stored = sem("x_stored")
        x_back = [sem(f"x_back{i}") for i in range(4)]
        out_t = sem("out_t")
        out_ready = [sem(f"out_ready{i}") for i in range(2)]
        out_stored = [sem(f"out_stored{i}") for i in range(2)]

        C_A0 = 0
        C_O0 = C_A0 + SWA_IN
        C_F0 = C_O0 + KD
        C_A1 = C_F0 + 2 * FT + KD * len(FF_GROUPS)
        C_O1 = C_A1 + FOX_IN
        C_F1 = C_O1 + KD
        C_END = C_F1 + 2 * FT + KD * len(FF_GROUPS)

        def wait(eng, s, value):
            if not (isinstance(value, int) and value <= 0):
                eng.wait_ge(s, value)

        def ff_phases(c0):
            c, t, found = c0, 0, []
            for n in FF_GROUPS:
                found.append((c, c + 2 * n, t, n))
                c, t = c + 2 * n + KD, t + n
            return found

        def out_bank(t):
            b = (0, 2, 6)[t % 3]
            return psum[:, b * HALF:b * HALF + D]

        def half(h):
            return slice(h * HALF, (h + 1) * HALF)

        def apart(eng):
            eng.nop(nofuse=True)

        block = ctx.enter_context(nc.Block())

        class Attention:
            def __init__(self, name):
                self.fox = name == "fox"
                self.units = FOX_H if self.fox else SWA_KV
                self.qk, self.v = (fox_qk, fox_v) if self.fox else (swa_qk, swa_v)
                self.qk_dmas, self.v_dmas = (5, 2) if self.fox else (5, 4)
                self.qk_in = [sem(f"{name}_qk_in{e}") for e in range(2)]
                self.v_in = [sem(f"{name}_v_in{e}") for e in range(2)]
                self.qk_done = sem(f"{name}_qk_done")
                self.max_done = sem(f"{name}_max_done")
                self.exp_done = sem(f"{name}_exp_done")
                self.sum_done = sem(f"{name}_sum_done")
                self.inv_done = sem(f"{name}_inv_done")
                self.norm_done = sem(f"{name}_norm_done")
                self.t_done = sem(f"{name}_t_done")
                self.ph_done = sem(f"{name}_ph_done")
                self.t_free = sem(f"{name}_t_free")
                self.pv_done = sem(f"{name}_pv_done")
                self.oh_done = sem(f"{name}_oh_done")
                self.o_free = sem(f"{name}_o_free")
                self.tiles = [(0, 1), (2, 3), (4,), (5,), (6,), (7,)] if self.fox else [(t,) for t in range(TT)]
                self.steps = len(self.tiles)
                self.rings = 6 if self.fox else 4
                self.ahead = dict(qk=4, scores=4, exps=3, inverse=3, norm=3) if self.fox else \
                    dict(qk=3, scores=3, exps=2, inverse=1, norm=1)
                self.blocks = [[[(0, 0, 1), (1, 0, 2)]], [[(2, 0, 3)], [(3, 0, 4)]]] + \
                    [[[(t, 0, 4)], [(t, 4, t - 3)]] for t in range(4, TT)] if self.fox else [[1]] + [[0, 1]] * (TT - 1)
                self.fills = [len(b) for b in self.blocks]
                self.unit_fills = sum(self.fills)
                self.groups = TT // 2 if self.fox else TT
                n = 2 * self.unit_fills
                self.turns = [T_BANKS[i % 3] for i in range(n)]
                if n % 3 == 1:
                    self.turns[-1] = T_BANKS[1]

            def count(self, u, s):
                return self.steps * u + s

            def ring(self, e, s):
                return (self.steps * e + s) % self.rings

            def fill(self, u, s):
                return self.unit_fills * u + sum(self.fills[:s])

            def bank_of(self, u, e, s, j):
                f = self.fill(u if isinstance(u, int) else e, s) + j
                n = len(self.turns)
                ago = next(d for d in range(1, n) if self.turns[(f - d) % n] == self.turns[f % n])
                return bank[self.turns[f % n]], ago

            def group(self, s):
                return self.tiles[s][-1] // 2 if self.fox else s

            def completes(self, s):
                return not self.fox or self.tiles[s][-1] % 2 == 1

        T_BANKS = (4, 5, 7)
        O_BANK = 6
        swa, fox = Attention("swa"), Attention("fox")
        cum_in = [sem(f"fox_cum_in{e}") for e in range(2)]
        fox_moved = sem("fox_moved")
        fox_joined = sem("fox_joined")
        swa_row = sem("swa_row")
        N_CONST = 7
        NEWTON_STEPS = 6
        GATE_STEPS = 14

        def a_step(a, pi, i, last):
            if i < 2 * a.steps:
                return 2 * pi + i // a.steps, i // a.steps, i % a.steps
            return None if last else (2 * pi + 2, 0, i - 2 * a.steps)

        def a_done(a, pi, i, first):
            if i < 0:
                return None
            if i == 0:
                return None if first else (2 * pi - 1, 1, a.steps - 1, pi - 1)
            e, s = (i - 1) // a.steps, (i - 1) % a.steps
            return (2 * pi + e, e, s, pi) if a.completes(s) else None

        def rows(e):
            return slice(e * HD, (e + 1) * HD)

        def fox_w(t):
            return (t + 1) * P

        def fox_at(t):
            return {1: P, 3: HALF}.get(t, 0)

        def fox_pieces(blocks, tb, p):
            at0, found = 0, []
            for t, k, n in blocks:
                found.append((p[:, k:k + n, t % 2 * P:t % 2 * P + P],
                              tb[:, at0:at0 + n * P].rearrange("p (b q) -> p b q", q=P)))
                at0 += n * P
            return found

        def fox_operands(u, e):
            if isinstance(u, int) and u == 0:
                return fox_first
            return [b[e] for b in (fox_q_hi, fox_q_lo, fox_k, fox_values)]

        w_in_view = {"swa": swa_w_in[0].rearrange("(k p) n -> p k n", p=P),
                     "fox": fox_w_in[0].rearrange("(k p) n -> p k n", p=P)}
        w_out_view = {"swa": swa_w_out[0].rearrange("(k p) n -> p k n", p=P),
                      "fox": fox_w_out[0].rearrange("(k p) n -> p k n", p=P)}
        gu_view = [w_gate_up[i].rearrange("(k p) n -> p k n", p=P) for i in range(2)]
        dn_view = [w_down[i].rearrange("(k p) n -> p k n", p=P) for i in range(2)]
        x_view = x[0].rearrange("(t p) d -> t p d", p=P)
        out_view = out[0].rearrange("(t p) d -> t p d", p=P)

        @block.sync
        def _(sp):
            def load_w(c, p, src, n=KD):
                wait(sp, w_split, c - 1)
                sp.dma_start(w_raw[p][:, 0:n, :], src).then_inc(w_loaded[p], 16)

            def strip(view, m):
                return view[:, :, bass.ds(m * P, P)]

            def load_out_w(c0, view, i):
                for p in range(2):
                    load_w(c0 + 2 * i + p, p, strip(view, 2 * i + p))

            def load_qk(a, u, e):
                hi, lo = a.qk
                wait(sp, a.qk_done, a.steps * (u - 1))
                if a.fox:
                    q_hi, q_lo, k = fox_operands(u, e)[:3]
                    for r in range(2):
                        sp.dma_start(q_hi[rows(r), :].bitcast(FP32), hi[bass.ds(u * HD, HD), :]).then_inc(a.qk_in[e], 16)
                        sp.dma_start(k[rows(r), :].bitcast(FP32), a.qk[r][bass.ds((FOX_H + u) * HD, HD), :])\
                            .then_inc(a.qk_in[e], 16)
                    sp.dma_start(q_lo[rows(0), :].bitcast(FP32), lo[bass.ds(u * HD, HD), :]).then_inc(a.qk_in[e], 16)
                    wait(sp, a.max_done, a.steps * (u - 1))
                    sp.dma_start(cum_all[e][:, :], cum_scr[bass.ds(u, 1), :].to_broadcast([P, SEQ])).then_inc(cum_in[e], 16)
                    return
                load_q(a, u, e)
                load_k(a, u, e)

            def load_q(a, u, e):
                for r in range(2):
                    sp.dma_start(swa_q[e][rows(r), :, :].bitcast(FP32),
                                 a.qk[r][2 * u * P:(2 * u + 2) * P, :].rearrange("(g p) n -> p g n", p=HD))\
                        .then_inc(a.qk_in[e], 16)

            def load_k(a, u, e):
                at0 = slice((SWA_Q + u) * HD, (SWA_Q + u + 1) * HD)
                for r in range(2):
                    sp.dma_start(swa_k_hi[e][rows(r), :].bitcast(FP32), a.qk[0][at0, :]).then_inc(a.qk_in[e], 16)
                sp.dma_start(swa_k_lo[e][rows(0), :].bitcast(FP32), a.qk[1][at0, :]).then_inc(a.qk_in[e], 16)

            def load_v(a, u, e, pi):
                wait(sp, a.pv_done, a.groups * (u - 1))
                if a.fox:
                    for r in range(2):
                        sp.dma_start(fox_operands(u, e)[3][:, :, rows(r)].bitcast(FP32),
                                     a.v[r][bass.ds(pi * P, P), :, rows(e)])\
                            .then_inc(a.v_in[e], 16)
                    return
                for src, dst in zip(a.v, (v_hi, v_lo)):
                    for r in range(2):
                        sp.dma_start(dst[e][:, :, rows(r)].bitcast(FP32), src[u // 2 * P:(u // 2 + 1) * P, :, rows(u % 2)])\
                            .then_inc(a.v_in[e], 16)

            def load_unit(a, u, e, pi):
                load_qk(a, u, e)
                load_v(a, u, e, pi)

            def load_ffn(layer, c0):
                for cg, cd, t0, n in ff_phases(c0):
                    with sp.Fori(0, n) as j:
                        load_w(cg + 2 * j, 0, strip(gu_view[layer], t0 + j))
                        load_w(cg + 2 * j + 1, 1, strip(gu_view[layer], FT + t0 + j))
                    with sp.Fori(0, KD // 2) as i:
                        for p in range(2):
                            load_w(cd + 2 * i + p, p,
                                   dn_view[layer][:, t0:t0 + n, bass.ds((2 * i + p) * P, P)], n)

            def attention_loads(a):
                if a.fox:
                    sp.wait_ge(gate_stored, 16)
                    sp.wait_ge(stored[0], 16 * SWA_IN + 32 * (FOX_H + 2) // 2)
                    load_unit(a, 0, 0, 0)
                else:
                    sp.wait_ge(stored[0], 16 * (SWA_Q // 2 + 2))
                    load_k(a, 0, 0)
                sp.wait_ge(mm_done, 2 * (C_O1 if a.fox else C_O0))
                for p in range(2):
                    sp.wait_ge(stored[p], 16 * (SWA_IN + (FOX_IN if a.fox else 0)))
                if not a.fox:
                    load_v(a, 0, 0, 0)
                load_unit(a, 1, 1, 0)
                if a.fox:
                    with sp.Fori(1, a.units // 2) as pi:
                        for e in range(2):
                            load_unit(a, 2 * pi + e, e, pi)
                else:
                    for u in range(2, a.units):
                        load_unit(a, u, u % 2, u // 2)
                k = 2 if a.fox else 0
                sp.wait_ge(a.pv_done, a.groups * a.units - 1)
                sp.dma_start(x_t[:, 0:2, :], x_scr[:, 0:2, :]).then_inc(x_back[k], 16)
                for t0, t1 in ((2, 4), (4, 6), (6, KD)):
                    if t0 == (4 if a.fox else 2):
                        sp.wait_ge(a.pv_done, a.groups * a.units)
                    sp.dma_start(x_t[:, t0:t1, :], x_scr[:, t0:t1, :]).then_inc(x_back[k + 1], 16)

            sp.dma_start(ident[:, :], masks[:, 0:P]).then_inc(ident_in, 16)
            for t in range(TT):
                if t >= 4:
                    sp.wait_ge(xin_t, t - 3)
                sp.dma_start(start_x[t % 4][:, :], x_view[t]).then_inc(xin_loaded[t % 4], 16)
                if t == 3:
                    load_w(0, 0, strip(w_in_view["swa"], 0))
                if t == 7:
                    load_w(1, 1, strip(w_in_view["swa"], 1))
            sp.dma_start(rope_cos[:, :], rope[0]).then_inc(rope_in, 16)
            sp.dma_start(rope_sin[:, :], rope[1]).then_inc(rope_in, 16)

            with sp.Fori(1, SWA_IN // 2) as i:
                for p in range(2):
                    load_w(2 * i + p, p, strip(w_in_view["swa"], 2 * i + p))
            sp.wait_ge(x_stored, 16)
            for p in range(2):
                sp.wait_ge(stored[p], 32)
            load_q(swa, 0, 0)
            load_out_w(C_O0, w_out_view["swa"], 0)
            attention_loads(swa)
            with sp.Fori(1, KD // 2) as i:
                load_out_w(C_O0, w_out_view["swa"], i)
            load_ffn(0, C_F0)

            load_w(C_A1, 0, strip(w_in_view["fox"], 0))
            load_w(C_A1 + 1, 1, strip(w_in_view["fox"], 1))
            sp.wait_ge(mm_done, 2 * C_A1)
            f0 = 3 * FOX_H * HD
            sp.dma_start(wf_raw[:, :, :], w_in_view["fox"][:, :, f0:f0 + FOX_H]).then_inc(gate_in, 16)
            sp.dma_start(f_bias[:, :], fox_f_bias.rearrange("a h -> h a"), allow_slow_non_contiguous=True).then_inc(gate_in, 16)
            with sp.Fori(1, FOX_IN // 2) as i:
                for p in range(2):
                    load_w(C_A1 + 2 * i + p, p, strip(w_in_view["fox"], 2 * i + p))
            load_out_w(C_O1, w_out_view["fox"], 0)
            attention_loads(fox)
            with sp.Fori(1, KD // 2) as i:
                load_out_w(C_O1, w_out_view["fox"], i)
            load_ffn(1, C_F1)
            for t in range(0, TT, 2):
                sp.wait_ge(out_ready[0], t // 2 + 1)
                sp.dma_start(out_view[t], out_tile[t][:, :]).then_inc(out_stored[0], 16)
            for p in range(2):
                sp.wait_ge(out_stored[p], 16 * TT // 2)

        @block.gpsimd
        def _(pool):
            nc.gpsimd.memset(ones[:, :], 1.0).then_inc(ones_ready, 1)

            def norm_probs(a, u, e, s):
                n = a.count(u, s)
                sl = a.ring(e, s)
                pool.wait_ge(a.inv_done, n + 1)
                if a.fox:
                    for i, t in enumerate(a.tiles[s]):
                        sc = score[sl][:, fox_at(t):fox_at(t) + fox_w(t)]
                        last = nc.gpsimd.tensor_tensor(sc, sc, inv_l[sl][:, i:i + 1].to_broadcast([P, fox_w(t)]),
                                                       ALU.mult)
                    last.then_inc(a.norm_done, 1)
                else:
                    w0 = 0 if s else P
                    sc = score[sl][:, :].rearrange("p (g w) -> p g w", g=GQ)[:, :, w0:]
                    nc.gpsimd.tensor_tensor(sc, sc, inv_l[sl][:, :].unsqueeze(2).to_broadcast([P, GQ, 2 * P - w0]),
                                            ALU.mult).then_inc(a.norm_done, 1)

            def pair_norms(a, pi, last):
                for i in range(2 * a.steps):
                    if ahead := a_step(a, pi, i + a.ahead["norm"], last):
                        norm_probs(a, *ahead)

            def attention(a):
                for s in range(a.ahead["norm"]):
                    norm_probs(a, 0, 0, s)
                pair_norms(a, 0, False)
                if a.fox:
                    with pool.Fori(1, a.units // 2 - 1) as pi:
                        pair_norms(a, pi, False)
                pair_norms(a, a.units // 2 - 1, True)

            def sum_squares(c0, k):
                def pair(i, first):
                    for p in range(2):
                        for h in range(2):
                            n = 16 * k + 4 * i + 2 * p + h
                            pool.wait_ge(sq_done, n + 1)
                            wait(pool, sq_used, n)
                            if first and p == 0:
                                nc.gpsimd.tensor_copy(ssq[:, half(h)], sq[h][:, :]).then_inc(sq_used, 1)
                            else:
                                nc.gpsimd.tensor_tensor(ssq[:, half(h)], ssq[:, half(h)], sq[h][:, :], ALU.add)\
                                    .then_inc(sq_used, 1)
                pair(0, True)
                with pool.Fori(1, KD // 2) as i:
                    pair(i, False)

            def rope_cosine(c):
                pool.wait_ge(evac_done, 2 * c + 2)
                wait(pool, c_ready, c)
                nc.gpsimd.tensor_tensor(rope_part[:, :], work_a[:, :], rope_cos[:, :], ALU.mult).then_inc(cos_done, 1)
            for t in range(TT):
                pool.wait_ge(start_copy, t + 1)
                xs = x_t[:, :, t * P:(t + 1) * P]
                nc.gpsimd.tensor_tensor(start_sq[:, :, t * P:(t + 1) * P], xs, xs, ALU.mult).then_inc(start_square, 1)
            pool.wait_ge(rope_in, 32)
            rope_cosine(0)
            with pool.Fori(1, SWA_IN - 2) as c:
                rope_cosine(c)
            attention(swa)
            sum_squares(C_O0, 0)
            sum_squares(0, 1)
            attention(fox)
            sum_squares(0, 2)
            sum_squares(0, 3)

        @block.scalar
        def _(act):
            def high(c, p):
                act.wait_ge(w_loaded[p], 8 * (c - p) + 16)
                wait(act, mm_done, 2 * c - 2)
                nc.scalar.activation(w_hi[p][:, :, :], w_raw[p][:, :, :], ACT.Copy).then_inc(w_high, 1)

            def norm_root(k):
                act.wait_ge(nat_done, k + 1)

                nc.scalar.activation(nat_y[:, :], bank[5][:, 0:TT], ACT.Sqrt, bias=eps_c[:, :], scale=1.0 / D)\
                    .then_inc(sd_done, 1)

            def norm_spread(k):
                for h in range(2):
                    act.wait_ge(bc_done, 2 * k + h + 1)
                    nc.scalar.activation(rstd[:, half(h)], bank[6 + h], ACT.Copy).then_inc(rstd_ready, 1)

            def part_high_of(p, before, scale, s, value):
                act.wait_ge(s, value)
                wait(act, stored[p], 16 * (before - p))
                nc.scalar.activation(part_hi[p][:, :], work_c[:, :], ACT.Copy, scale=scale).then_inc(part_high, 1)

            def value_high_of(p, before, t_before):
                act.wait_ge(stored[p], 16 * (before - p))
                for h in range(2):
                    act.wait_ge(part_t, 2 * t_before + h + 1)
                    nc.scalar.activation(part_hi[p][:, half(h)], bank[4 + h], ACT.Copy).then_inc(value_high, 1)

            def store_part(p, before, dst, m):
                act.wait_ge(part_low, before + 1)
                for t, d in ((part_hi, dst[0]), (part_lo, dst[1])):
                    act.dma_start(d[bass.ds(m * P, P), :], t[p][:, :].bitcast(FP32)).then_inc(stored[p], 16)

            def store_value(p, before, dst, m):
                act.wait_ge(part_low, before + 1)
                for t, d in ((part_hi, dst[0]), (part_lo, dst[1])):
                    act.dma_start(d[bass.ds(m * P, P), :, :].rearrange("p t d -> p (t d)"), t[p][:, :].bitcast(FP32))\
                        .then_inc(stored[p], 16)

            def exps(a, u, e, s):
                n = a.count(u, s)
                sl = a.ring(e, s)
                act.wait_ge(a.max_done, n + 1)
                if a.fox:
                    for i, t in enumerate(a.tiles[s]):
                        sc = score[sl][:, fox_at(t):fox_at(t) + fox_w(t)]
                        last = nc.scalar.activation(sc, sc, ACT.Exp, bias=neg_max[sl][:, i:i + 1], scale=-1.0,
                                                    accum_out=psum_l[sl][:, i:i + 1])
                    last.then_inc(a.exp_done, 1)
                    return
                for g in range(GQ):
                    w0 = 0 if s else P
                    at0 = s % 2 * SEQ + g % 2 * HALF + g // 2 * 2 * P
                    nc.scalar.activation(score[sl][:, g * 2 * P + w0:(g + 1) * 2 * P], psum[:, at0 + w0:at0 + 2 * P],
                                         ACT.Exp, bias=neg_max[sl][:, g:g + 1], scale=-SCALE,
                                         accum_out=psum_l[sl][:, g:g + 1])
                nc.scalar.activation(sink_e[sl][:, :], sink_e[sl][:, :], ACT.Exp).then_inc(a.exp_done, 1)

            def probs_high(a, u, e, s):
                g = a.group(s)
                par = g % 2
                wait(act, a.pv_done, a.groups * u + g - 1)
                for j, blocks in enumerate(a.blocks[s]):
                    f = a.fill(u, s) + j
                    tb = a.bank_of(u, e, s, j)[0]
                    act.wait_ge(a.t_done, f + 1)
                    if a.fox:
                        for dst, src in fox_pieces(blocks, tb, fox_p_hi[par]):
                            last = nc.scalar.activation(dst, src, ACT.Copy)
                        last.then_inc(a.ph_done, 1)
                    else:
                        nc.scalar.activation(swa_p_hi[par][:, blocks, :], tb, ACT.Copy).then_inc(a.ph_done, 1)

            def result_high(a, u, e, s, pi):
                g = a.group(s)
                pb = bank[O_BANK]
                if a.fox:
                    act.wait_ge(fox_joined, a.groups * u + g + 1)
                    apart(act)
                    nc.scalar.activation(o_hi[rows(e), bass.ds(pi, 1), 2 * P * g:2 * P * (g + 1)],
                                         joint[g % 2][rows(e), :].unsqueeze(1), ACT.Copy).then_inc(a.oh_done, 1)
                else:
                    act.wait_ge(a.pv_done, a.groups * u + g + 1)
                    for r in range(2):
                        last = nc.scalar.activation(
                            o_hi[rows(r), 2 * u:2 * u + 2, s * P:(s + 1) * P],
                            pb.rearrange("p (a b q) -> p a b q", a=2, b=2)[rows(r), :, r, :], ACT.Copy)
                    last.then_inc(a.oh_done, 1)

            def move(a, u, e, s, pi):
                g = a.group(s)
                act.wait_ge(a.pv_done, a.groups * u + g + 1)
                nc.scalar.activation(v_low_part[g % 2][rows(0), :], bank[O_BANK][rows(1), 0:2 * P], ACT.Copy)\
                    .then_inc(fox_moved, 1)

            def pair_act(a, pi, first, last):
                for i in range(2 * a.steps):
                    u, e, s = a_step(a, pi, i, last)
                    probs_high(a, u, e, s)
                    if ahead := a_step(a, pi, i + a.ahead["exps"], last):
                        exps(a, *ahead)
                    if done := a_done(a, pi, i - 1 if a.fox else i, first):
                        result_high(a, *done)
                    if a.fox and (done := a_done(a, pi, i, first)):
                        move(a, *done)
                if last:
                    if a.fox:
                        move(a, 2 * pi + 1, 1, a.steps - 1, pi)
                    result_high(a, 2 * pi + 1, 1, a.steps - 1, pi)

            def attention(a):
                for s in range(a.ahead["exps"]):
                    exps(a, 0, 0, s)
                pair_act(a, 0, True, False)
                if a.fox:
                    with act.Fori(1, a.units // 2 - 1) as pi:
                        pair_act(a, pi, False, False)
                pair_act(a, a.units // 2 - 1, False, True)

            def update(c0, k, store=False, final=False):
                def pair(i, ahead=True):
                    for p in range(2):
                        c = c0 + 2 * i + p
                        m = 2 * i + p
                        for h in range(2):
                            n = 16 * k + 4 * i + 2 * p + h
                            act.wait_ge(evac_done, 2 * c + h + 1)
                            apart(act)
                            xs = x_t[:, bass.ds(m, 1), half(h)]
                            dst = (x_fin if final else h_hi)[:, bass.ds(m, 1), half(h)]
                            nc.scalar.activation(dst, xs, ACT.Copy, scale=gains[:, k + 1, bass.ds(m, 1)])\
                                .then_inc(hi_done, 1)
                            wait(act, sq_used, n - 1)
                            apart(act)
                            nc.scalar.activation(sq[h][:, :].unsqueeze(1), xs, ACT.Square).then_inc(sq_done, 1)
                        if store:
                            act.dma_start(x_scr[:, bass.ds(m, 1), :], x_t[:, bass.ds(m, 1), :]).then_inc(x_stored, 16)
                        if ahead:
                            high(c + 2, p)
                pair(0)
                if final:
                    with act.Fori(1, KD // 2 - 1) as i:
                        pair(i)
                    pair(KD // 2 - 1, False)
                else:
                    with act.Fori(1, KD // 2) as i:
                        pair(i)

            def ffn(layer, c0, k):
                for gi, (cg, cd, t0, n) in enumerate(ff_phases(c0)):
                    def pair(j):
                        tile = FT * layer + t0 + j
                        for h in range(2):
                            act.wait_ge(evac_done, 2 * (cg + 2 * j) + h + 1)
                            nc.scalar.activation(work_a[:, half(h)], work_a[:, half(h)], ACT.Silu)\
                                .then_inc(silu_done, 1)
                        high(cg + 2 * j + 2, 0)
                        for h in range(2):
                            act.wait_ge(prod_done, 2 * tile + h + 1)
                            apart(act)
                            nc.scalar.activation(hid_hi[:, bass.ds(j, 1), half(h)], work_b[:, half(h)].unsqueeze(1),
                                                 ACT.Copy).then_inc(hid_hi_done, 1)
                        high(cg + 2 * j + 3, 1)
                    if gi == 0:
                        norm_root(k)
                        norm_spread(k)
                        pair(0)
                        with act.Fori(1, n) as j:
                            pair(j)
                    else:
                        with act.Fori(0, n) as j:
                            pair(j)
                    if gi < len(FF_GROUPS) - 1:
                        with act.Fori(0, KD // 2) as i:
                            for p in range(2):
                                high(cd + 2 * i + p + 2, p)

            act.dma_start(gains[:, 0:1, :], norm_mix[0:1].rearrange("a (k p) -> p a k", p=P), allow_slow_non_contiguous=True).then_inc(gain_in, 16)
            act.dma_start(band[:, :], masks[:, P:3 * P]).then_inc(const_in, 16)
            act.dma_start(causal[:, :], masks[:, 3 * P:4 * P]).then_inc(const_in, 16)
            act.dma_start(gains[:, 1:2, :], norm_ffn[0:1].rearrange("a (k p) -> p a k", p=P), allow_slow_non_contiguous=True).then_inc(const_in, 16)
            act.dma_start(gains[:, 2:3, :], norm_mix[1:2].rearrange("a (k p) -> p a k", p=P), allow_slow_non_contiguous=True).then_inc(const_in, 16)
            act.dma_start(gains[:, 3:4, :], norm_ffn[1:2].rearrange("a (k p) -> p a k", p=P), allow_slow_non_contiguous=True).then_inc(const_in, 16)
            act.dma_start(gains[:, 4:5, :], norm_final.rearrange("(a k p) -> p a k", a=1, p=P), allow_slow_non_contiguous=True).then_inc(const_in, 16)
            act.dma_start(sinks[:, :], swa_sinks.to_broadcast([P, SWA_Q])).then_inc(const_in, 16)

            def start_high(t):
                act.wait_ge(start_gain, t + 1)
                nc.scalar.activation(h_hi[:, :, t * P:(t + 1) * P], start_h[t % 2][:, :, :], ACT.Copy)\
                    .then_inc(start_hi, 1)
            for t in range(TT):
                ps = psum[:, t % 2 * D:(t % 2 + 1) * D].rearrange("p (k q) -> p k q", q=P)
                act.wait_ge(xin_t, t + 1)
                nc.scalar.activation(x_t[:, :, t * P:(t + 1) * P], ps, ACT.Copy).then_inc(start_copy, 1)
                if t > 0:
                    start_high(t - 1)
                if t == 6:
                    high(0, 0)
            start_high(TT - 1)
            high(1, 1)
            act.wait_ge(start_copy, TT)
            act.dma_start(x_scr[:, :, :], x_t[:, :, :]).then_inc(x_stored, 16)
            norm_root(0)
            norm_spread(0)

            def swa_rope_pair(i, scale, first=False):
                for p in range(2):
                    c = 2 * i + p
                    high(c + 2, p)
                    if not (first and p == 0):
                        store_part(1 - p, c - 1, swa_qk, c - 1)
                    part_high_of(p, c, scale, c_ready, c + 1)
            swa_rope_pair(0, -1.0, True)
            with act.Fori(1, 4) as i:
                swa_rope_pair(i, -1.0)
            swa_rope_pair(4, 1.0)
            high(12, 0)
            store_part(1, 9, swa_qk, 9)
            nc.scalar.activation(warm[:, :], eps_c[:, :], ACT.Exp)
            value_high_of(0, 10, 0)
            high(13, 1)
            store_value(0, 10, swa_v, 0)
            value_high_of(1, 11, 1)
            store_value(1, 11, swa_v, 1)
            act.wait_ge(x_stored, 16)
            attention(swa)
            update(C_O0, 0)
            ffn(0, C_F0, 1)
            update(ff_phases(C_F0)[-1][1], 1, store=True)
            norm_root(2)
            norm_spread(2)
            act.wait_ge(gate_in, 32)
            nc.scalar.activation(wf_hi[:, :, :], wf_raw[:, :, :], ACT.Copy).then_inc(gate_w, 1)

            def fox_in_pair(i, scale, first=False):
                for p in range(2):
                    m = 2 * i + p
                    c = C_A1 + m
                    high(c + 2, p)
                    if not (first and p == 0):
                        store_part(1 - p, SWA_IN + m - 1, fox_qk, m - 1)
                    part_high_of(p, SWA_IN + m, scale, evac_done, 2 * c + 2)
            fox_in_pair(0, -1.0, True)
            act.wait_ge(gate_v, 4)
            nc.scalar.activation(gate[3][:, :], gate[2][:, :], ACT.Exp).then_inc(gate_a, 1)
            act.wait_ge(gate_v, 5)
            nc.scalar.activation(gate[5][:, :], gate[4][:, :], ACT.Ln).then_inc(gate_a, 1)
            with act.Fori(1, 4) as i:
                fox_in_pair(i, -1.0)
            act.wait_ge(gate_v, GATE_STEPS)
            act.dma_start(cum_scr[:, :], gate[7][:, :]).then_inc(gate_stored, 16)
            with act.Fori(4, 8) as i:
                fox_in_pair(i, 1.0)

            def value_pair(i, first=False):
                for p in range(2):
                    m = 2 * i + p
                    high(C_A1 + 16 + m + 2, p)
                    if first and p == 0:
                        store_part(1, SWA_IN + 15, fox_qk, 15)
                    else:
                        store_value(1 - p, SWA_IN + 16 + m - 1, fox_v, m - 1)
                    value_high_of(p, SWA_IN + 16 + m, 2 + m)
            nc.scalar.activation(warm[:, :], eps_c[:, :], ACT.Exp)
            value_pair(0, True)
            with act.Fori(1, 4) as i:
                value_pair(i)
            store_value(1, SWA_IN + FOX_IN - 1, fox_v, FOX_H // 2 - 1)
            act.wait_ge(x_stored, 16 * (KD + 1))
            attention(fox)
            update(C_O1, 2)
            ffn(1, C_F1, 3)
            update(ff_phases(C_F1)[-1][1], 3, final=True)
            norm_root(4)
            act.wait_ge(newton, NEWTON_STEPS * 5)
            for t in range(1, TT, 2):
                act.wait_ge(out_t, t + 1)
                nc.scalar.activation(out_tile[t][:, :], out_bank(t), ACT.Copy, scale=nat_y[:, t:t + 1])\
                    .then_inc(out_ready[1], 1)
                act.wait_ge(out_ready[1], t // 2 + 1)
                act.dma_start(out_view[t], out_tile[t][:, :]).then_inc(out_stored[1], 16)

        @block.vector
        def _(dve):
            V = nc.vector

            def low(c, p):
                dve.wait_ge(w_high, c + 1)
                V.tensor_tensor(w_lo[p][:, :, :], w_raw[p][:, :, :], w_hi[p][:, :, :].bitcast(FP32), ALU.subtract)\
                    .then_inc(w_split, 1)

            newton_at = [0]

            def step(ins):
                newton_at[0] += 1
                ins.then_inc(newton, 1)
                dve.wait_ge(newton, newton_at[0])

            def norm_factor(k):
                dve.wait_ge(sd_done, k + 1)
                step(V.tensor_scalar(nat_v[:, :], bank[5][:, 0:TT], 1.0 / D, EPS, ALU.mult, ALU.add))
                step(V.reciprocal(nat_y[:, :], nat_y[:, :]))
                step(V.tensor_tensor(nat_t[:, :], nat_y[:, :], nat_y[:, :], ALU.mult))
                step(V.tensor_tensor(nat_t[:, :], nat_t[:, :], nat_v[:, :], ALU.mult))
                step(V.tensor_scalar(nat_t[:, :], nat_t[:, :], -0.5, 1.5, ALU.mult, ALU.add))
                step(V.tensor_tensor(nat_y[:, :], nat_y[:, :], nat_t[:, :], ALU.mult))
                assert newton_at[0] == NEWTON_STEPS * (k + 1)

            def norm_diag(k):
                norm_factor(k)
                V.tensor_tensor(diag[:, :, :], ident[:, :].unsqueeze(1).to_broadcast([P, TT, P]),
                                nat_y[:, :].unsqueeze(2).to_broadcast([P, TT, P]), ALU.mult).then_inc(diag_done, 1)

            def scale_half(c, h, dst, src):
                dve.wait_ge(mm_done, 2 * c + h + 1)
                V.tensor_tensor(dst[:, half(h)], src, rstd[:, half(h)], ALU.mult).then_inc(evac_done, 1)

            def part_low_of(p, n, scale):
                dve.wait_ge(part_high, n + 1)
                V.scalar_tensor_tensor(out=part_lo[p][:, :], in0=work_c[:, :], scalar=scale,
                                       in1=part_hi[p][:, :].bitcast(FP32), op0=ALU.mult, op1=ALU.subtract)\
                    .then_inc(part_low, 1)

            def value_strip(c, p, before, t_before):
                dve.wait_ge(part_low, before)
                for h in range(2):
                    scale_half(c, h, work_c, bank[2 * p + h])
                low(c + 2, p)
                for h in range(2):
                    dve.wait_ge(value_high, 2 * t_before + h + 1)
                    last = V.tensor_tensor(part_lo[p][:, half(h)], bank[4 + h], part_hi[p][:, half(h)].bitcast(FP32),
                                           ALU.subtract)
                last.then_inc(part_low, 1)

            def scores(a, u, e, s):
                n = a.count(u, s)
                sl = a.ring(e, s)
                ps = psum[:, s % 2 * SEQ:(s % 2 + 1) * SEQ]
                dve.wait_ge(a.qk_done, n + 1)
                if a.fox:
                    if s == 0:
                        dve.wait_ge(cum_in[e], 8 * (u - e) + 16)
                    apart(dve)
                    for i, t in enumerate(a.tiles[s]):
                        here = slice(fox_at(t), fox_at(t) + fox_w(t))
                        last = V.tensor_tensor_reduce(out=score[sl][:, here], in0=ps[:, here],
                                                      in1=cum_all[e][:, 0:fox_w(t)],
                                                      scale=SCALE, scalar=3.0e38, op0=ALU.add, op1=ALU.min,
                                                      accum_out=neg_max[sl][:, i:i + 1])
                    last.then_inc(a.max_done, 1)
                    return
                V.tensor_reduce(neg_max[sl][:, :].rearrange("p (a r) -> p a r", a=2),
                                ps.rearrange("p (r a w) -> p a r w", r=2, a=2)[:, :, :, 0 if s else P:2 * P],
                                AX.X, ALU.min).then_inc(swa_row, 1)
                dve.wait_ge(swa_row, 2 * n + 1)
                V.scalar_tensor_tensor(out=neg_max[sl][:, :], in0=neg_max[sl][:, :], scalar=SCALE,
                                       in1=sinks[:, GQ * u:GQ * (u + 1)], op0=ALU.mult, op1=ALU.min).then_inc(swa_row, 1)
                dve.wait_ge(swa_row, 2 * (n + 1))
                V.tensor_tensor(sink_e[sl][:, :], neg_max[sl][:, :], sinks[:, GQ * u:GQ * (u + 1)], ALU.subtract)\
                    .then_inc(a.max_done, 1)

            def inverse(a, u, e, s):
                n = a.count(u, s)
                sl = a.ring(e, s)
                dve.wait_ge(a.exp_done, n + 1)
                if a.fox:
                    m = len(a.tiles[s])
                    V.reciprocal(inv_l[sl][:, 0:m], psum_l[sl][:, 0:m]).then_inc(a.inv_done, 1)
                else:
                    V.tensor_tensor(psum_l[sl][:, :], psum_l[sl][:, :], sink_e[sl][:, :], ALU.add)\
                        .then_inc(a.sum_done, 1)
                    dve.wait_ge(a.sum_done, n + 1)
                    V.reciprocal(inv_l[sl][:, :], psum_l[sl][:, :]).then_inc(a.inv_done, 1)

            def probs_low(a, u, e, s):
                par = a.group(s) % 2
                for j, blocks in enumerate(a.blocks[s]):
                    f = a.fill(u, s) + j
                    tb = a.bank_of(u, e, s, j)[0]
                    dve.wait_ge(a.ph_done, f + 1)
                    if a.fox:
                        for (dst, src), (high_part, _) in zip(fox_pieces(blocks, tb, fox_p_lo[par]),
                                                              fox_pieces(blocks, tb, fox_p_hi[par])):
                            last = V.tensor_tensor(dst, src, high_part.bitcast(FP32), ALU.subtract)
                        last.then_inc(a.t_free, 1)
                    else:
                        V.tensor_tensor(swa_p_lo[par][:, blocks, :], tb, swa_p_hi[par][:, blocks, :].bitcast(FP32),
                                        ALU.subtract).then_inc(a.t_free, 1)

            def result_low(a, u, e, s, pi):
                g = a.group(s)
                pb = bank[O_BANK]
                dve.wait_ge(a.oh_done, a.groups * u + g + 1)
                if a.fox:
                    at0 = (rows(e), bass.ds(pi, 1), slice(2 * P * g, 2 * P * (g + 1)))
                    V.tensor_tensor(o_lo[at0], joint[g % 2][rows(e), :].unsqueeze(1), o_hi[at0].bitcast(FP32),
                                    ALU.subtract).then_inc(a.o_free, 1)
                else:
                    for r in range(2):
                        at0 = (rows(r), slice(2 * u, 2 * u + 2), slice(s * P, (s + 1) * P))
                        last = V.tensor_tensor(o_lo[at0],
                                               pb.rearrange("p (a b q) -> p a b q", a=2, b=2)[rows(r), :, r, :],
                                               o_hi[at0].bitcast(FP32), ALU.subtract)
                    last.then_inc(a.o_free, 1)

            def join(a, u, e, s, pi):
                g = a.group(s)
                dve.wait_ge(fox_moved, a.groups * u + g + 1)
                wait(dve, a.o_free, a.groups * u + g - 1)
                V.tensor_tensor(joint[g % 2][rows(e), :], bank[O_BANK][rows(0), 0:2 * P], v_low_part[g % 2][rows(0), :],
                                ALU.add).then_inc(fox_joined, 1)

            def pair_dve(a, pi, first, last):
                for i in range(2 * a.steps):
                    u, e, s = a_step(a, pi, i, last)
                    if not a.fox and (ahead := a_step(a, pi, i + a.ahead["inverse"], last)):
                        inverse(a, *ahead)
                    probs_low(a, u, e, s)
                    if ahead := a_step(a, pi, i + a.ahead["scores"], last):
                        scores(a, *ahead)
                    if a.fox and (ahead := a_step(a, pi, i + a.ahead["inverse"], last)):
                        inverse(a, *ahead)
                    if done := a_done(a, pi, i - 1 if a.fox else i, first):
                        result_low(a, *done)
                    if a.fox and (done := a_done(a, pi, i, first)):
                        join(a, *done)
                if last:
                    if a.fox:
                        join(a, 2 * pi + 1, 1, a.steps - 1, pi)
                    result_low(a, 2 * pi + 1, 1, a.steps - 1, pi)

            def attention(a):
                late = a.ahead["scores"] - a.ahead["inverse"]
                for s in range(a.ahead["scores"]):
                    scores(a, 0, 0, s)
                    if s >= late:
                        inverse(a, 0, 0, s - late)
                pair_dve(a, 0, True, False)
                if a.fox:
                    with dve.Fori(1, a.units // 2 - 1) as pi:
                        pair_dve(a, pi, False, False)
                pair_dve(a, a.units // 2 - 1, False, True)

            def update(c0, k, back=None, ahead_last=True, final=False, plain=False):
                def pair(i, ahead=True, back_sem=None):
                    if back_sem is not None:
                        dve.wait_ge(back_sem, 16)
                    for p in range(2):
                        c = c0 + 2 * i + p
                        m = 2 * i + p
                        for h in range(2):
                            dve.wait_ge(mm_done, 2 * c + h + 1)
                            xs = x_t[:, bass.ds(m, 1), half(h)]
                            V.tensor_tensor(xs, bank[2 * p + h].unsqueeze(1), xs, ALU.add).then_inc(evac_done, 1)
                        if not (plain or final):
                            for h in range(2):
                                n = 16 * k + 4 * i + 2 * p + h
                                dve.wait_ge(hi_done, n + 1)
                                xs = x_t[:, bass.ds(m, 1), half(h)]
                                V.scalar_tensor_tensor(out=h_lo[:, bass.ds(m, 1), half(h)], in0=xs,
                                                       scalar=gains[:, k + 1, bass.ds(m, 1)],
                                                       in1=h_hi[:, bass.ds(m, 1), half(h)].bitcast(FP32),
                                                       op0=ALU.mult, op1=ALU.subtract).then_inc(h_ready, 1)
                        if ahead:
                            low(c + 2, p)
                pair(0, back_sem=x_back[back] if back is not None else None)
                if back is not None:
                    dve.wait_ge(x_back[back + 1], 48)
                if final:
                    with dve.Fori(1, KD // 2 - 1) as i:
                        pair(i)
                    pair(KD // 2 - 1, False)
                else:
                    with dve.Fori(1, KD // 2) as i:
                        pair(i)

            def ffn(layer, c0, k):
                for gi, (cg, cd, t0, n) in enumerate(ff_phases(c0)):
                    def pair(j):
                        tile = FT * layer + t0 + j
                        c = cg + 2 * j
                        if not (isinstance(tile, int) and tile == 0):
                            dve.wait_ge(prod_done, 2 * tile)
                        for h in range(2):
                            scale_half(c, h, work_a, bank[h])
                        low(c + 2, 0)
                        if not (isinstance(tile, int) and tile == 0):
                            dve.wait_ge(hid_ready, 2 * tile)
                        for h in range(2):
                            scale_half(c + 1, h, work_b, bank[2 + h])
                        for h in range(2):
                            dve.wait_ge(silu_done, 2 * tile + h + 1)
                            dve.wait_ge(evac_done, 2 * (c + 1) + h + 1)
                            V.tensor_tensor(work_b[:, half(h)], work_b[:, half(h)], work_a[:, half(h)], ALU.mult)\
                                .then_inc(prod_done, 1)
                        for h in range(2):
                            dve.wait_ge(hid_hi_done, 2 * tile + h + 1)
                            V.tensor_tensor(hid_lo[:, bass.ds(j, 1), half(h)], work_b[:, half(h)].unsqueeze(1),
                                            hid_hi[:, bass.ds(j, 1), half(h)].bitcast(FP32), ALU.subtract)\
                                .then_inc(hid_ready, 1)
                        low(c + 3, 1)
                    if gi == 0:
                        norm_diag(k)
                        dve.wait_ge(rstd_ready, 2 * k + 2)
                        pair(0)
                        with dve.Fori(1, n) as j:
                            pair(j)
                    else:
                        with dve.Fori(0, n) as j:
                            pair(j)
                    if gi < len(FF_GROUPS) - 1:
                        update(cd, None, plain=True)

            V.memset(eps_c[:, :], EPS)

            def start_low(t):
                dve.wait_ge(start_hi, t + 1)
                V.tensor_tensor(h_lo[:, :, t * P:(t + 1) * P], start_h[t % 2][:, :, :],
                                h_hi[:, :, t * P:(t + 1) * P].bitcast(FP32), ALU.subtract).then_inc(h_ready, 1)
            dve.wait_ge(gain_in, 16)
            for t in range(TT):
                dve.wait_ge(start_copy, t + 1)
                wait(dve, h_ready, t - 1)
                V.tensor_tensor(start_h[t % 2][:, :, :], x_t[:, :, t * P:(t + 1) * P],
                                gains[:, 0, :].unsqueeze(2).to_broadcast([P, KD, P]), ALU.mult).then_inc(start_gain, 1)
                if t > 0:
                    start_low(t - 1)
                if t == 6:
                    low(0, 0)
            start_low(TT - 1)
            low(1, 1)
            for t in range(TT):
                dve.wait_ge(start_square, t + 1)
                V.tensor_reduce(ssq[:, t * P:(t + 1) * P], start_sq[:, :, t * P:(t + 1) * P].rearrange("p k q -> p q k"),
                                AX.X, ALU.add).then_inc(start_sum, 1)
            dve.wait_ge(const_in, 16 * N_CONST)
            V.tensor_copy(ident_bf[:, :], ident[:, :]).then_inc(const_ready, 1)
            V.tensor_copy(causal_bf[:, :], causal[:, :]).then_inc(const_ready, 1)
            V.tensor_copy(band_bf[:, :], band[:, :]).then_inc(const_ready, 1)
            V.tensor_scalar(sinks[:, :], sinks[:, :], -1.0, None, ALU.mult).then_inc(const_ready, 1)
            norm_diag(0)
            dve.wait_ge(rstd_ready, 2)

            def swa_rope_strip(c, p, first=False, before=-1.0):
                if not first:
                    dve.wait_ge(c_ready, c)
                scale_half(c, 0, work_a, bank[2 * p])
                if not first:
                    part_low_of(1 - p, c - 1, before)
                scale_half(c, 1, work_a, bank[2 * p + 1])
                low(c + 2, p)
                dve.wait_ge(evac_done, 2 * c + 2)
                for b in range(4):
                    last = V.tensor_copy(work_b[32 * b:32 * b + 32, :], work_a[32 * (b ^ 1):32 * (b ^ 1) + 32, :])
                last.then_inc(swapped, 1)
                dve.wait_ge(swapped, c + 1)
                if first:
                    dve.wait_ge(rope_in, 32)
                V.tensor_tensor(work_b[:, :], work_b[:, :], rope_sin[:, :], ALU.mult).then_inc(sin_done, 1)
                dve.wait_ge(sin_done, c + 1)
                dve.wait_ge(cos_done, c + 1)
                if not first:
                    dve.wait_ge(part_low, c)
                V.tensor_tensor(work_c[:, :], rope_part[:, :], work_b[:, :], ALU.add).then_inc(c_ready, 1)
            swa_rope_strip(0, 0, True)
            swa_rope_strip(1, 1)
            with dve.Fori(1, 4) as i:
                for p in range(2):
                    swa_rope_strip(2 * i + p, p)
            swa_rope_strip(8, 0)
            swa_rope_strip(9, 1, before=1.0)
            dve.wait_ge(c_ready, SWA_IN - 2)
            part_low_of(1, SWA_IN - 3, 1.0)
            for p in range(2):
                value_strip(10 + p, p, 10 + p, p)
            attention(swa)
            update(C_O0, 0, back=0)
            ffn(0, C_F0, 1)
            update(ff_phases(C_F0)[-1][1], 1)
            norm_diag(2)
            dve.wait_ge(rstd_ready, 6)
            dve.wait_ge(gate_w, 1)
            V.tensor_tensor(wf_lo[:, :, :], wf_raw[:, :, :], wf_hi[:, :, :].bitcast(FP32), ALU.subtract)\
                .then_inc(gate_w, 1)

            def fox_in_strip(m, p, scale=-1.0):
                dve.wait_ge(part_low, SWA_IN + m)
                for h in range(2):
                    scale_half(C_A1 + m, h, work_c, bank[2 * p + h])
                low(C_A1 + m + 2, p)
                part_low_of(p, SWA_IN - 2 + m, scale)
            fox_in_strip(0, 0)
            fox_in_strip(1, 1)
            G = [g[:, :] for g in gate]
            gate_at = [0]

            def gate_step(ins):
                gate_at[0] += 1
                ins.then_inc(gate_v, 1)
                dve.wait_ge(gate_v, gate_at[0])
            dve.wait_ge(gate_mm, 1)
            gate_step(V.tensor_tensor(G[0], psum[0:FOX_H, 4 * HALF:6 * HALF], rstd[0:FOX_H, :], ALU.mult))
            gate_step(V.tensor_scalar(G[0], G[0], f_bias[:, :], None, ALU.add))
            gate_step(V.tensor_scalar(G[1], G[0], -1.0, None, ALU.mult))
            gate_step(V.tensor_tensor(G[2], G[0], G[1], ALU.min))
            dve.wait_ge(gate_a, 1)
            gate_step(V.tensor_scalar(G[4], G[3], 1.0, None, ALU.add))
            gate_step(V.tensor_scalar(G[1], G[4], -1.0, None, ALU.add))
            gate_step(V.tensor_tensor(G[1], G[3], G[1], ALU.subtract))
            dve.wait_ge(gate_a, 2)
            fox_in_strip(2, 0)
            gate_step(V.reciprocal(G[6], G[4]))
            fox_in_strip(3, 1)
            gate_step(V.tensor_tensor(G[1], G[1], G[6], ALU.mult))
            gate_step(V.tensor_tensor(G[5], G[5], G[1], ALU.add))
            gate_step(V.tensor_scalar(G[0], G[0], 0.0, 1.0 / SCALE, ALU.min, ALU.mult))
            gate_step(V.scalar_tensor_tensor(out=G[5], in0=G[5], scalar=-1.0 / SCALE, in1=G[0],
                                             op0=ALU.mult, op1=ALU.add))
            gate_step(V.memset(G[2], 1.0))
            gate_step(V.tensor_tensor_scan(G[7], G[2], G[5], 0.0, ALU.mult, ALU.add))
            assert gate_at[0] == GATE_STEPS, gate_at
            with dve.Fori(2, 4) as i:
                for p in range(2):
                    fox_in_strip(2 * i + p, p)
            with dve.Fori(4, 8) as i:
                for p in range(2):
                    fox_in_strip(2 * i + p, p, 1.0)
            with dve.Fori(0, 4) as i:
                for p in range(2):
                    m = 2 * i + p
                    value_strip(C_A1 + 16 + m, p, SWA_IN + 16 + m, 2 + m)
            attention(fox)
            update(C_O1, 2, back=2)
            ffn(1, C_F1, 3)
            update(ff_phases(C_F1)[-1][1], 3, final=True)
            norm_factor(4)
            for t in range(0, TT, 2):
                dve.wait_ge(out_t, t + 1)
                V.tensor_scalar(out_tile[t][:, :], out_bank(t), nat_y[:, t:t + 1], None, ALU.mult)\
                    .then_inc(out_ready[0], 1)

        @block.tensor
        def _(pe):
            T = nc.tensor

            def chunk(c, p, n, mh, ml, ready=None, after=None):
                pe.wait_ge(w_split, c + 1)
                for h in range(2):
                    wait(pe, evac_done, 2 * c + h - 3)
                    for k in range(n):
                        if ready:
                            ready(h, k)
                        T.matmul(bank[2 * p + h], w_hi[p][:, k, :], mh[:, k, half(h)], start=k == 0, stop=False)
                        T.matmul(bank[2 * p + h], w_hi[p][:, k, :], ml[:, k, half(h)], start=False, stop=False)
                        last = T.matmul(bank[2 * p + h], w_lo[p][:, k, :], mh[:, k, half(h)], start=False,
                                        stop=k == n - 1)
                    last.then_inc(mm_done, 1)
                    if after:
                        after(h)

            def norm_sums(k):
                if k == 0:
                    pe.wait_ge(start_sum, TT)
                else:
                    pe.wait_ge(sq_used, 16 * k)
                for t in range(TT):
                    last = T.matmul(bank[5][:, t:t + 1], ssq[:, t * P:(t + 1) * P], ones[:, 0:1], start=True, stop=True)
                last.then_inc(nat_done, 1)

            def norm_bc(k):
                pe.wait_ge(diag_done, k + 1)
                for h in range(2):
                    T.matmul(bank[6 + h], ones[:, :], diag[:, 4 * h:4 * h + 4, :], start=True, stop=True)\
                        .then_inc(bc_done, 1)

            def linear(c0, pairs, n, mh, ml, ready=None, norm=None):
                def after0(h):
                    if norm is not None and h == (1 if norm == 0 else 0):
                        norm_sums(norm)

                def after1(h):
                    if norm is not None and h == 0:
                        norm_bc(norm)
                chunk(c0, 0, n, mh, ml, ready, after0)
                chunk(c0 + 1, 1, n, mh, ml, None, after1)

            def values_t(c, before):
                pe.wait_ge(evac_done, 2 * c + 2)
                for h in range(2):
                    pe.wait_ge(part_low, before)
                    for b in range(4):
                        last = T.transpose(bank[4 + h][:, b * P:(b + 1) * P], work_c[:, (4 * h + b) * P:(4 * h + b + 1) * P],
                                           ident[:, :])
                    last.then_inc(part_t, 1)

            def value_chunks(c0, pairs, before):
                def pair(i, first):
                    for p in range(2):
                        c = c0 + 2 * i + p
                        n = before + 2 * i + p

                        def after(h):
                            if h == 0 and not (first and p == 0):
                                values_t(c - 1, n - 1)
                        chunk(c, p, KD, h_hi, h_lo, None, after)
                pair(0, True)
                if pairs > 1:
                    with pe.Fori(1, pairs) as i:
                        pair(i, False)
                values_t(c0 + 2 * pairs - 1, before + 2 * pairs - 1)

            def linear_rest(c0, pairs, n, mh, ml, first=1):
                with pe.Fori(first, pairs) as i:
                    for p in range(2):
                        chunk(c0 + 2 * i + p, p, n, mh, ml)

            def h_wait(base):
                def ready(h, k):
                    pe.wait_ge(h_ready, base + 2 * k + h + 1)
                return ready

            def qk(a, u, e, s):
                n = a.count(u, s)
                at0 = s % 2 * SEQ
                wait(pe, a.max_done if a.fox else a.exp_done, n - 1)
                if s == 0:
                    pe.wait_ge(a.qk_in[e], 8 * a.qk_dmas * (u - e + 2))
                if a.fox:
                    q_hi, q_lo, key = fox_operands(u, e)[:3]
                    for t in a.tiles[s]:
                        qs, w = slice(t * P, (t + 1) * P), fox_w(t)
                        for cc in range(0, w, HALF):
                            ww = min(HALF, w - cc)
                            ps = psum[:, at0 + fox_at(t) + cc:at0 + fox_at(t) + cc + ww]
                            diagonal = cc + ww == w
                            T.matmul(ps, q_hi[:, qs], key[:, cc:cc + ww], start=True, stop=False)
                            last = T.matmul(ps, q_lo[rows(0), qs], key[rows(0), cc:cc + ww], start=False,
                                            stop=not diagonal)
                            if diagonal:
                                last = T.matmul(ps[:, ww - P:ww], ident_bf[:, :], causal_bf[:, :], start=False,
                                                stop=True)
                else:
                    qs = slice(s * P, (s + 1) * P)
                    k0 = (s - 1) * P if s else 0
                    w0 = 0 if s else P
                    for g in range(GQ):
                        ps = bank[s % 2 * 2 + g % 2][:, g // 2 * 2 * P + w0:(g // 2 + 1) * 2 * P]
                        T.matmul(ps, swa_q[e][:, g, qs], swa_k_hi[e][:, k0:(s + 1) * P], start=True, stop=False)
                        T.matmul(ps, swa_q[e][rows(0), g, qs], swa_k_lo[e][rows(0), k0:(s + 1) * P], start=False,
                                 stop=False)
                        last = T.matmul(ps, ident_bf[:, :], band_bf[:, w0:2 * P], start=False, stop=True)
                last.then_inc(a.qk_done, 1)

            def transposes(a, u, e, s):
                n = a.count(u, s)
                sl = a.ring(e, s)
                pe.wait_ge(a.norm_done, n + 1)
                for j, blocks in enumerate(a.blocks[s]):
                    f = a.fill(u, s) + j
                    tb, ago = a.bank_of(u, e, s, j)
                    wait(pe, a.t_free, f - ago + 1)
                    if a.fox:
                        sources = [fox_at(t) + (k + b) * P for t, k, n in blocks for b in range(n)]
                    else:
                        sources = [b * 2 * P + blocks * P for b in range(GQ)]
                    for b, at0 in enumerate(sources):
                        last = T.transpose(tb[:, b * P:(b + 1) * P], score[sl][:, at0:at0 + P], ident[:, :])
                    last.then_inc(a.t_done, 1)

            def pv(a, u, e, s, pi):
                g = a.group(s)
                par, t = g % 2, a.tiles[s][-1]
                pb = bank[O_BANK]
                pe.wait_ge(a.t_free, a.fill(u, s) + a.fills[s])
                wait(pe, fox_joined if a.fox else a.o_free, a.groups * u + g)
                if g == 0:
                    pe.wait_ge(a.v_in[e], 8 * a.v_dmas * (u - e + 2))
                if a.fox:
                    terms = [(k, k, slice(0 if k < t else P, 2 * P)) for k in range(t + 1)]
                    ph, pl, v = fox_p_hi[par], fox_p_lo[par], fox_operands(u, e)[3]
                    for i, (vt, pt, cs) in enumerate(terms):
                        T.matmul(pb[:, cs], v[:, vt, :], ph[:, pt, cs], start=i == 0, stop=False)
                        last = T.matmul(pb[:, cs], v[:, vt, :], pl[:, pt, cs], start=False, stop=i == len(terms) - 1)
                else:
                    terms = [(t - 1 + j, j, slice(0, HALF)) for j in range(0 if t else 1, 2)]
                    ph, pl, vh, vl = swa_p_hi[par], swa_p_lo[par], v_hi[e], v_lo[e]
                    for i, (vt, pt, cs) in enumerate(terms):
                        T.matmul(pb[:, cs], vh[:, vt, :], ph[:, pt, cs], start=i == 0, stop=False)
                        T.matmul(pb[:, cs], vh[:, vt, :], pl[:, pt, cs], start=False, stop=False)
                        last = T.matmul(pb[:, cs], vl[:, vt, :], ph[:, pt, cs], start=False,
                                        stop=i == len(terms) - 1)
                last.then_inc(a.pv_done, 1)

            def out_first(a, h, ks, begin):
                c0 = C_O1 if a.fox else C_O0
                for k in ks:
                    T.matmul(bank[h], w_hi[0][:, k, :], o_hi[:, k, half(h)], start=begin and k == 0, stop=False)
                    T.matmul(bank[h], w_hi[0][:, k, :], o_lo[:, k, half(h)], start=False, stop=False)
                    last = T.matmul(bank[h], w_lo[0][:, k, :], o_hi[:, k, half(h)], start=False, stop=k == KD - 1)
                return last

            def out_early(a, i):
                if i < 2 * a.steps - 2:
                    return
                if i == 2 * a.steps - 2:
                    pe.wait_ge(w_split, (C_O1 if a.fox else C_O0) + 1)
                pe.wait_ge(a.o_free, a.groups * (a.units - (2 if a.fox else 1)))
                pe.wait_ge(a.exp_done, a.steps * a.units - 1)
                out_first(a, 0, range(2) if i == 2 * a.steps - 2 else range(2, early_tiles(a)), True)

            def early_tiles(a):
                return KD - (1 if a.fox else 2)

            def pair_pe(a, pi, first, last):
                for i in range(2 * a.steps):
                    u, e, s = a_step(a, pi, i, last)
                    transposes(a, u, e, s)
                    if last:
                        out_early(a, i)
                    if ahead := a_step(a, pi, i + a.ahead["qk"], last):
                        qk(a, *ahead)
                    if done := a_done(a, pi, i, first):
                        pv(a, *done)
                if last:
                    pv(a, 2 * pi + 1, 1, a.steps - 1, pi)

            def attention(a):
                pe.wait_ge(const_ready, 4)
                pe.wait_ge(evac_done, 2 * (C_O1 if a.fox else C_O0))
                pe.wait_ge(rstd_ready, 6 if a.fox else 2)
                for s in range(a.ahead["qk"]):
                    qk(a, 0, 0, s)
                pair_pe(a, 0, True, False)
                if a.fox:
                    with pe.Fori(1, a.units // 2 - 1) as pi:
                        pair_pe(a, pi, False, False)
                pair_pe(a, a.units // 2 - 1, False, True)

            def out_projection(a, c0):
                out_first(a, 1, range(early_tiles(a)), True)
                pe.wait_ge(a.o_free, a.groups * a.units)
                for h in range(2):
                    out_first(a, h, range(early_tiles(a), KD), False).then_inc(mm_done, 1)
                chunk(c0 + 1, 1, KD, o_hi, o_lo)
                linear_rest(c0, KD // 2, KD, o_hi, o_lo)

            def ffn(layer, c0, h_base, k):
                for gi, (cg, cd, t0, n) in enumerate(ff_phases(c0)):
                    if gi == 0:
                        linear(cg, n, KD, h_hi, h_lo, h_wait(h_base), norm=k)
                        linear_rest(cg, n, KD, h_hi, h_lo)
                    else:
                        linear_rest(cg, n, KD, h_hi, h_lo, first=0)

                    def hid_wait(h, kk, t0=t0):
                        pe.wait_ge(hid_ready, 2 * (FT * layer + t0 + kk) + h + 1)
                    linear(cd, KD // 2, n, hid_hi, hid_lo, hid_wait)
                    linear_rest(cd, KD // 2, n, hid_hi, hid_lo)

            pe.wait_ge(ident_in, 16)
            pe.wait_ge(ones_ready, 1)
            for t in range(TT):
                pe.wait_ge(xin_loaded[t % 4], 16 * (t // 4 + 1))
                if t >= 2:
                    pe.wait_ge(start_copy, t - 1)
                for k in range(KD):
                    at0 = t % 2 * D + k * P
                    last = T.transpose(psum[:, at0:at0 + P], start_x[t % 4][:, k * P:(k + 1) * P], ident[:, :])
                last.then_inc(xin_t, 1)
            pe.wait_ge(start_copy, TT)

            def start_wait(h, k):
                if k == 0:
                    pe.wait_ge(h_ready, 4 * h + 4)
            linear(C_A0, SWA_IN // 2, KD, h_hi, h_lo, start_wait, norm=0)
            linear_rest(C_A0, 5, KD, h_hi, h_lo)
            value_chunks(C_A0 + 10, 1, SWA_IN - 2)
            attention(swa)
            out_projection(swa, C_O0)
            ffn(0, C_F0, TT, 1)
            linear(C_A1, FOX_IN // 2, KD, h_hi, h_lo, h_wait(TT + 2 * KD), norm=2)
            pe.wait_ge(gate_w, 2)
            for h in range(2):
                for k in range(KD):
                    dst = bank[4 + h][0:FOX_H, :]
                    T.matmul(dst, wf_hi[:, k, :], h_hi[:, k, half(h)], start=k == 0, stop=False)
                    T.matmul(dst, wf_hi[:, k, :], h_lo[:, k, half(h)], start=False, stop=False)
                    last = T.matmul(dst, wf_lo[:, k, :], h_hi[:, k, half(h)], start=False, stop=k == KD - 1)
            last.then_inc(gate_mm, 1)
            linear_rest(C_A1, 8, KD, h_hi, h_lo)
            value_chunks(C_A1 + 16, 4, SWA_IN + 16)
            attention(fox)
            out_projection(fox, C_O1)
            ffn(1, C_F1, TT + 4 * KD, 3)
            pe.wait_ge(hi_done, 64)
            pe.wait_ge(evac_done, 2 * C_END)
            for t in range(TT):
                if t == 3:
                    norm_sums(4)
                if t >= 3:
                    pe.wait_ge(out_ready[(t - 3) % 2], (t - 3) // 2 + 1)
                for k in range(KD):
                    last = T.transpose(out_bank(t)[:, k * P:(k + 1) * P], x_fin[:, k, t * P:(t + 1) * P], ident[:, :])
                last.then_inc(out_t, 1)


_INS = ["x", "norm_mix", "norm_ffn", "swa_w_in", "swa_sinks", "swa_w_out", "fox_w_in", "fox_f_bias", "fox_w_out",
        "ffn_w_gate_up", "ffn_w_down", "norm_final"]


def _constants():
    half_d = HD // 2
    inv_freq = (10000.0 ** (-np.arange(half_d, dtype=np.float64) / half_d)).astype(np.float32)
    ang = (np.arange(SEQ, dtype=np.float32)[None, :] * inv_freq[:, None]).astype(np.float64)
    cos, sin = np.cos(ang), np.sin(ang)
    rope = np.stack([np.concatenate([cos] * 4), np.concatenate([-sin, sin] * 2)]).astype(np.float32)
    q, k = np.arange(P)[:, None], np.arange(P)[None, :]
    previous = np.where(k // CHUNK >= q // CHUNK + 1, 0.0, BIG)
    own = np.where(k // CHUNK <= q // CHUNK, 0.0, BIG)
    causal = np.where(k <= q, 0.0, BIG)
    masks = np.concatenate([np.eye(P), previous, own, causal], axis=1).astype(np.float32)
    return rope, masks


def kernel(**inputs):
    import concourse.bacc as bacc
    from concourse.bass_utils import run_bass_kernel_spmd

    nc = bacc.Bacc("TRN2", target_bir_lowering=False, num_devices=1)
    rope, masks = _constants()
    arrays, args = {}, {}
    for name in _INS:
        a = np.ascontiguousarray(inputs[name])
        arrays[f"in_{name}"] = a
        args[name] = nc.dram_tensor(f"in_{name}", a.shape, mybir.dt.from_np(a.dtype), kind="ExternalInput").ap()
    for name, a in (("rope", rope), ("masks", masks)):
        arrays[f"in_{name}"] = a
        args[name] = nc.dram_tensor(f"in_{name}", a.shape, FP32, kind="ExternalInput").ap()
    out = nc.dram_tensor("out_0", (1, SEQ, D), FP32, kind="ExternalOutput").ap()
    trunk(nc, args["x"], args["norm_mix"], args["norm_ffn"], args["swa_w_in"], args["swa_sinks"],
          args["swa_w_out"], args["fox_w_in"], args["fox_f_bias"], args["fox_w_out"], args["ffn_w_gate_up"],
          args["ffn_w_down"], args["norm_final"], args["rope"], args["masks"], out)
    r = run_bass_kernel_spmd(nc, [arrays], core_ids=[0])
    return r.results[0]["out_0"]
```
